# Optimizing a Trainium2 kernel written in Bass

```python
import math
import jax, jax.numpy as jnp
from jax import lax
import numpy as np

D_MODEL = 1024
BATCH = 1
SEQ = 512
DEPTH = 2

MEM_TOKENS = 256
GRID_W = 64
A_HEADS = 4
A_HEAD_DIM = D_MODEL // 8
A_WIDTH = A_HEADS * A_HEAD_DIM
A_CONV = 5
A_CHUNK = 128
B_HEADS = 8
B_HEAD_DIM = D_MODEL // 16
B_WIDTH = B_HEADS * B_HEAD_DIM
NA_ROWS = 8
NA_COLS = 16
C_HEADS = 8
C_HEAD_DIM = D_MODEL // 16
C_WIDTH = C_HEADS * 2 * C_HEAD_DIM
Q_BLOCK = 128
X_HEADS = 4
X_HEAD_DIM = D_MODEL // X_HEADS
FFN_HIDDEN = -(-8 * D_MODEL // (3 * 256)) * 256
ROPE_THETA = 10000.0
LN_EPS = 1e-5
DEEPNORM_ALPHA = (2 * DEPTH) ** 0.25
DEEPNORM_BETA = (8 * DEPTH) ** -0.25
N_EVEN = (DEPTH + 1) // 2
N_ODD = DEPTH // 2
EVEN_IN = 4 * A_WIDTH + 4 * A_HEADS + 3 * B_WIDTH
STATE_NEG = -1e30


def layer_norm(x, g, b):
    xf = x.astype(jnp.float32)
    mu = jnp.mean(xf, axis=-1, keepdims=True)
    var = jnp.mean(jnp.square(xf - mu), axis=-1, keepdims=True)
    return ((xf - mu) * lax.rsqrt(var + LN_EPS)).astype(x.dtype) * g + b

def rms_norm(x, g):
    xf = x.astype(jnp.float32)
    y = xf * lax.rsqrt(jnp.mean(jnp.square(xf), axis=-1, keepdims=True) + LN_EPS)
    return y.astype(x.dtype) * g

def split_cols(t, widths):
    offs = np.cumsum(widths)[:-1].tolist()
    return jnp.split(t, offs, axis=-1)

def centred_depthwise_conv(x, w):
    K, C = w.shape
    return lax.conv_general_dilated(
        x, w.reshape(K, 1, C).astype(x.dtype), window_strides=(1,),
        padding=[(K // 2, K // 2)], dimension_numbers=('NWC', 'WIO', 'NWC'),
        feature_group_count=C)

def rope(t):
    S, d = t.shape[1], t.shape[-1]
    inv_freq = ROPE_THETA ** (-jnp.arange(0, d, 2, dtype=jnp.float32) / d)
    ang = jnp.arange(S, dtype=jnp.float32)[:, None] * inv_freq[None, :]
    cos = jnp.cos(ang)[:, None, :]
    sin = jnp.sin(ang)[:, None, :]
    tf = t.astype(jnp.float32)
    t1, t2 = tf[..., : d // 2], tf[..., d // 2:]
    return jnp.concatenate([t1 * cos - t2 * sin, t1 * sin + t2 * cos], axis=-1).astype(t.dtype)

def mlstm_chunkwise(q, k, v, log_i, log_f):
    N, H, S, d = q.shape
    L = min(A_CHUNK, S)
    NC = S // L
    qc = q.reshape(N, H, NC, L, d)
    kc = k.reshape(N, H, NC, L, d)
    vc = v.reshape(N, H, NC, L, d)
    ai = log_i.reshape(N, H, NC, L)
    b = jnp.cumsum(log_f.reshape(N, H, NC, L), axis=-1)
    g = b[..., -1]
    w_end = g[..., None] - b + ai
    m_loc = jnp.max(w_end, axis=-1)
    p = jnp.exp(w_end - m_loc[..., None])
    kv_loc = jnp.einsum('nhcl,nhcld,nhcle->nhcde', p, kc, vc)
    k_loc = jnp.einsum('nhcl,nhcld->nhcd', p, kc)

    def step(carry, inp):
        C, nv, m = carry
        g_c, m_c, kv_c, k_c = inp
        m_new = jnp.maximum(g_c + m, m_c)
        s_old = jnp.exp(g_c + m - m_new)
        s_new = jnp.exp(m_c - m_new)
        C_new = s_old[..., None, None] * C + s_new[..., None, None] * kv_c
        n_new = s_old[..., None] * nv + s_new[..., None] * k_c
        return (C_new, n_new, m_new), (C, nv, m)

    init = (jnp.zeros((N, H, d, d), jnp.float32), jnp.zeros((N, H, d), jnp.float32),
            jnp.full((N, H), STATE_NEG, jnp.float32))
    xs = (jnp.moveaxis(g, 2, 0), jnp.moveaxis(m_loc, 2, 0),
          jnp.moveaxis(kv_loc, 2, 0), jnp.moveaxis(k_loc, 2, 0))
    _, (C_in, n_in, m_in) = lax.scan(step, init, xs)
    C_in = jnp.moveaxis(C_in, 0, 2)
    n_in = jnp.moveaxis(n_in, 0, 2)
    m_in = jnp.moveaxis(m_in, 0, 2)
    upto = jnp.tril(jnp.ones((L, L), dtype=bool))
    D = jnp.where(upto, b[..., :, None] - b[..., None, :] + ai[..., None, :], -jnp.inf)
    m_inter = b + m_in[..., None]
    m = jnp.maximum(jnp.max(D, axis=-1), m_inter)
    Smat = jnp.einsum('nhcld,nhcsd->nhcls', qc, kc) * jnp.exp(D - m[..., None])
    s_inter = jnp.exp(m_inter - m)
    num = (jnp.einsum('nhcls,nhcse->nhcle', Smat, vc)
           + s_inter[..., None] * jnp.einsum('nhcld,nhcde->nhcle', qc, C_in))
    den = jnp.sum(Smat, axis=-1) + s_inter * jnp.einsum('nhcld,nhcd->nhcl', qc, n_in)
    h = num / jnp.maximum(jnp.abs(den), jnp.exp(-m))[..., None]
    return h.reshape(N, H, S, d)

def neighbourhood_attention(q, k, v, rpb):
    B_, S, H, d = q.shape
    R = S // GRID_W
    kr = min(NA_ROWS, R)
    q = q.reshape(B_, R, GRID_W, H, d) * (d ** -0.5)
    k = k.reshape(B_, R, GRID_W, H, d)
    v = v.reshape(B_, R, GRID_W, H, d)
    rows = jnp.arange(R)
    row_start = jnp.clip(rows - NA_ROWS // 2, 0, R - kr)
    key_rows = row_start[:, None] + jnp.arange(kr)[None, :]
    k_blk = k[:, key_rows]
    v_blk = v[:, key_rows]
    cols = jnp.arange(GRID_W)
    col_start = jnp.clip(cols - NA_COLS // 2, 0, GRID_W - NA_COLS)
    in_win = (cols[None, :] >= col_start[:, None]) & (cols[None, :] < col_start[:, None] + NA_COLS)
    rel_r = key_rows - rows[:, None] + (NA_ROWS - 1)
    rel_c = jnp.clip(cols[None, :] - cols[:, None] + (NA_COLS - 1), 0, 2 * NA_COLS - 2)
    bias = rpb[:, rel_r[:, None, :, None], rel_c[None, :, None, :]]
    s = jnp.einsum('brqhd,brikhd->bhrqik', q, k_blk).astype(jnp.float32) + bias.astype(jnp.float32)
    s = jnp.where(in_win[:, None, :], s, -jnp.inf)
    p = jax.nn.softmax(s.reshape(B_, H, R, GRID_W, kr * GRID_W), axis=-1)
    p = p.reshape(B_, H, R, GRID_W, kr, GRID_W).astype(v.dtype)
    out = jnp.einsum('bhrqik,brikhd->brqhd', p, v_blk)
    return out.reshape(B_, S, H * d)

def diff_attention(q, k, v, lam):
    B_, S, H, _, d = q.shape
    nb = S // Q_BLOCK
    qb = jnp.moveaxis(q.reshape(B_, nb, Q_BLOCK, H, 2, d), 1, 0)
    scale = d ** -0.5

    def block(qi):
        s = jnp.einsum('bqhcd,bkhcd->bhcqk', qi, k).astype(jnp.float32) * scale
        p = jax.nn.softmax(s, axis=-1)
        a = p[:, :, 0] - lam * p[:, :, 1]
        return jnp.einsum('bhqk,bkhe->bqhe', a.astype(v.dtype), v)

    out = lax.map(block, qb)
    return jnp.moveaxis(out, 0, 1).reshape(B_, S, H, 2 * d)

def memory_cross_attention(x, mem, wq, wkv, wo):
    B_, S, _ = x.shape
    M = mem.shape[1]
    q = (x @ wq).reshape(B_, S, X_HEADS, X_HEAD_DIM) * (X_HEAD_DIM ** -0.5)
    k, v = jnp.split(mem @ wkv, 2, axis=-1)
    k = k.reshape(B_, M, X_HEADS, X_HEAD_DIM)
    v = v.reshape(B_, M, X_HEADS, X_HEAD_DIM)
    p = jax.nn.softmax(jnp.einsum('bshd,bmhd->bhsm', q, k).astype(jnp.float32), axis=-1)
    o = jnp.einsum('bhsm,bmhd->bshd', p.astype(v.dtype), v)
    return o.reshape(B_, S, D_MODEL) @ wo

def swiglu(x, w_gu, w_down):
    gate, up = jnp.split(x @ w_gu, 2, axis=-1)
    return (jax.nn.silu(gate) * up) @ w_down

def even_mixer(x, w_in, gate_b, conv_w, rpb, w_out):
    B_, S, _ = x.shape
    a_qk, a_v, a_o, a_g, b_q, b_k, b_v = split_cols(
        x @ w_in, [2 * A_WIDTH, A_WIDTH, A_WIDTH, 4 * A_HEADS, B_WIDTH, B_WIDTH, B_WIDTH])
    a_qk = jax.nn.silu(centred_depthwise_conv(a_qk, conv_w))
    a_q, a_k = jnp.split(a_qk, 2, axis=-1)

    def heads(t):
        return t.reshape(B_, S, A_HEADS, A_HEAD_DIM).transpose(0, 2, 1, 3).astype(jnp.float32)

    q, k, v = heads(a_q), heads(a_k) * (A_HEAD_DIM ** -0.5), heads(a_v)
    gates = (a_g.astype(jnp.float32) + gate_b.astype(jnp.float32)).reshape(B_, S, 4, A_HEADS).transpose(2, 0, 3, 1)

    def both_dirs(t):
        return jnp.concatenate([t, jnp.flip(t, axis=2)], axis=0)

    log_i = jnp.concatenate([gates[0], jnp.flip(gates[1], axis=-1)], axis=0)
    log_f = jax.nn.log_sigmoid(jnp.concatenate([gates[2], jnp.flip(gates[3], axis=-1)], axis=0))
    h2 = mlstm_chunkwise(both_dirs(q), both_dirs(k), both_dirs(v), log_i, log_f)
    h = h2[:B_] + jnp.flip(h2[B_:], axis=2)
    h = h.transpose(0, 2, 1, 3).reshape(B_, S, A_WIDTH).astype(x.dtype)
    a_out = jax.nn.sigmoid(a_o) * h
    b_out = neighbourhood_attention(b_q.reshape(B_, S, B_HEADS, B_HEAD_DIM),
                                    b_k.reshape(B_, S, B_HEADS, B_HEAD_DIM),
                                    b_v.reshape(B_, S, B_HEADS, B_HEAD_DIM), rpb)
    return jnp.concatenate([a_out, b_out], axis=-1) @ w_out

def odd_mixer(x, w_in, lam_p, subln_g, w_out, lam_init):
    B_, S, _ = x.shape
    q, k, v = jnp.split(x @ w_in, 3, axis=-1)
    q = rope(q.reshape(B_, S, 2 * C_HEADS, C_HEAD_DIM)).reshape(B_, S, C_HEADS, 2, C_HEAD_DIM)
    k = rope(k.reshape(B_, S, 2 * C_HEADS, C_HEAD_DIM)).reshape(B_, S, C_HEADS, 2, C_HEAD_DIM)
    v = v.reshape(B_, S, C_HEADS, 2 * C_HEAD_DIM)
    lp = lam_p.astype(jnp.float32)
    lam = jnp.exp(jnp.sum(lp[0] * lp[1])) - jnp.exp(jnp.sum(lp[2] * lp[3])) + lam_init
    o = diff_attention(q, k, v, lam)
    o = rms_norm(o, subln_g) * (1.0 - lam_init)
    return o.reshape(B_, S, C_WIDTH) @ w_out

def first_inputs(seed: int = 0) -> dict:
    key = jax.random.key(seed)
    ks = jax.random.split(key, 20)

    def nrm(kk, shape, scale):
        return jax.random.normal(kk, shape, jnp.float32) * scale

    x = nrm(ks[0], (BATCH, SEQ, D_MODEL), 1.0)
    mem = nrm(ks[1], (BATCH, MEM_TOKENS, D_MODEL), 1.0)
    even_w_in = nrm(ks[2], (N_EVEN, D_MODEL, EVEN_IN), D_MODEL ** -0.5)
    i_bias = nrm(ks[3], (N_EVEN, 2 * A_HEADS), 0.1)
    f_lin = jnp.linspace(3.0, 6.0, A_HEADS, dtype=jnp.float32)
    f_bias = jnp.concatenate([f_lin, f_lin])[None, :] + nrm(ks[4], (N_EVEN, 2 * A_HEADS), 0.1)
    even_gate_b = jnp.concatenate([i_bias, f_bias], axis=-1)
    even_conv_w = nrm(ks[5], (N_EVEN, A_CONV, 2 * A_WIDTH), A_CONV ** -0.5)
    even_rpb = nrm(ks[6], (N_EVEN, B_HEADS, 2 * NA_ROWS - 1, 2 * NA_COLS - 1), 0.02)
    even_w_out = nrm(ks[7], (N_EVEN, A_WIDTH + B_WIDTH, D_MODEL), (A_WIDTH + B_WIDTH) ** -0.5 * DEEPNORM_BETA)
    odd_w_in = nrm(ks[8], (N_ODD, D_MODEL, 3 * C_WIDTH), D_MODEL ** -0.5)
    odd_lambda = nrm(ks[9], (N_ODD, 4, C_HEAD_DIM), 0.1)
    odd_subln_g = 1.0 + nrm(ks[10], (N_ODD, 2 * C_HEAD_DIM), 0.02)
    odd_w_out = nrm(ks[11], (N_ODD, C_WIDTH, D_MODEL), C_WIDTH ** -0.5 * DEEPNORM_BETA)
    mem_wq = nrm(ks[12], (DEPTH, D_MODEL, D_MODEL), D_MODEL ** -0.5)
    mem_wkv = nrm(ks[13], (DEPTH, D_MODEL, 2 * D_MODEL), D_MODEL ** -0.5)
    mem_wo = nrm(ks[14], (DEPTH, D_MODEL, D_MODEL), D_MODEL ** -0.5 * DEEPNORM_BETA)
    ffn_w_gu = nrm(ks[15], (DEPTH, D_MODEL, 2 * FFN_HIDDEN), D_MODEL ** -0.5)
    ffn_w_down = nrm(ks[16], (DEPTH, FFN_HIDDEN, D_MODEL), FFN_HIDDEN ** -0.5 * DEEPNORM_BETA)
    ln_g = 1.0 + nrm(ks[17], (DEPTH, 3, D_MODEL), 0.02)
    ln_b = nrm(ks[18], (DEPTH, 3, D_MODEL), 0.02)
    return {'x': x, 'mem': mem, 'even_w_in': even_w_in, 'even_gate_b': even_gate_b,
            'even_conv_w': even_conv_w, 'even_rpb': even_rpb, 'even_w_out': even_w_out,
            'odd_w_in': odd_w_in, 'odd_lambda': odd_lambda, 'odd_subln_g': odd_subln_g,
            'odd_w_out': odd_w_out, 'mem_wq': mem_wq, 'mem_wkv': mem_wkv, 'mem_wo': mem_wo,
            'ffn_w_gu': ffn_w_gu, 'ffn_w_down': ffn_w_down, 'ln_g': ln_g, 'ln_b': ln_b}

def first_block(x, mem, even_w_in, even_gate_b, even_conv_w, even_rpb, even_w_out,
              odd_w_in, odd_lambda, odd_subln_g, odd_w_out, mem_wq, mem_wkv, mem_wo,
              ffn_w_gu, ffn_w_down, ln_g, ln_b):
    for layer in range(DEPTH):
        j = layer // 2
        if layer % 2 == 0:
            mix = even_mixer(x, even_w_in[j], even_gate_b[j], even_conv_w[j], even_rpb[j], even_w_out[j])
        else:
            lam_init = 0.8 - 0.6 * math.exp(-0.3 * layer)
            mix = odd_mixer(x, odd_w_in[j], odd_lambda[j], odd_subln_g[j], odd_w_out[j], lam_init)
        x = layer_norm(DEEPNORM_ALPHA * x + mix, ln_g[layer, 0], ln_b[layer, 0])
        xa = memory_cross_attention(x, mem, mem_wq[layer], mem_wkv[layer], mem_wo[layer])
        x = layer_norm(DEEPNORM_ALPHA * x + xa, ln_g[layer, 1], ln_b[layer, 1])
        ff = swiglu(x, ffn_w_gu[layer], ffn_w_down[layer])
        x = layer_norm(DEEPNORM_ALPHA * x + ff, ln_g[layer, 2], ln_b[layer, 2])
    return x


HALF = D_MODEL // 2
HGRN_HEADS = 4
HGRN_DIM = HALF // HGRN_HEADS
HGRN_CHUNK = 64
FOX_HEADS = 8
FOX_DIM = HALF // FOX_HEADS
LRU_WIDTH = HALF
LRU_BLOCKS = 8
LRU_BLOCK_DIM = LRU_WIDTH // LRU_BLOCKS
LRU_C = 8.0
CONV_WIDTH = 4
SB_HEADS = 8
SB_DIM = HALF // SB_HEADS
D_FF = -(-8 * D_MODEL // (3 * 256)) * 256
N_EVEN_2 = (DEPTH + 1) // 2
N_ODD_2 = DEPTH // 2
ALPHA = (2 * DEPTH) ** 0.25
BETA = (8 * DEPTH) ** -0.25
EVEN_IN_2 = 7 * HALF + FOX_HEADS
ODD_IN = 2 * LRU_WIDTH + 3 * HALF
EPS = 1e-5


def layer_norm_2(x, g, b):
    xf = x.astype(jnp.float32)
    mu = jnp.mean(xf, axis=-1, keepdims=True)
    xc = xf - mu
    var = jnp.mean(xc * xc, axis=-1, keepdims=True)
    y = xc * lax.rsqrt(var + EPS) * g.astype(jnp.float32) + b.astype(jnp.float32)
    return y.astype(x.dtype)

def rms_norm_f32(x, g):
    xf = x.astype(jnp.float32)
    return xf * lax.rsqrt(jnp.mean(xf * xf, axis=-1, keepdims=True) + EPS) * g.astype(jnp.float32)

def split_cols_2(t, sizes):
    return jnp.split(t, np.cumsum(sizes)[:-1].tolist(), axis=-1)

def hgrn2(q, f_logit, inp, g, lb, norm_g):
    B, S, _ = q.shape
    nc = S // HGRN_CHUNK
    z = f_logit.astype(jnp.float32)
    log_f = jnp.log(lb + (1.0 - lb) * jax.nn.sigmoid(z))
    k = (1.0 - lb) * jax.nn.sigmoid(-z)

    def to_chunks(t):
        return t.astype(jnp.float32).reshape(B, nc, HGRN_CHUNK, HGRN_HEADS, HGRN_DIM).transpose(1, 0, 3, 2, 4)

    qc, kc, vc, lc = to_chunks(q), to_chunks(k), to_chunks(inp), to_chunks(log_f)
    causal = jnp.tril(jnp.ones((HGRN_CHUNK, HGRN_CHUNK), dtype=bool))[:, :, None]

    def step(state, chunk):
        qt, kt, vt, lt = chunk
        b = jnp.cumsum(lt, axis=2)
        o_inter = jnp.einsum('bhtk,bhkv->bhtv', qt * jnp.exp(b), state)
        rel = b[:, :, :, None, :] - b[:, :, None, :, :]
        decay = jnp.exp(jnp.where(causal, rel, -jnp.inf))
        scores = jnp.einsum('bhtk,bhtsk,bhsk->bhts', qt, decay, kt)
        o = o_inter + jnp.einsum('bhts,bhsv->bhtv', scores, vt)
        b_last = b[:, :, -1:, :]
        state = jnp.exp(b_last[:, :, 0, :])[..., None] * state + jnp.einsum(
            'bhsk,bhsv->bhkv', kt * jnp.exp(b_last - b), vt)
        return state, o

    s0 = jnp.zeros((B, HGRN_HEADS, HGRN_DIM, HGRN_DIM), jnp.float32)
    _, o = lax.scan(step, s0, (qc, kc, vc, lc))
    o = o.transpose(1, 0, 3, 2, 4).reshape(B, S, HGRN_HEADS, HGRN_DIM)
    o = rms_norm_f32(o, norm_g)
    gate = jax.nn.silu(g.astype(jnp.float32)).reshape(B, S, HGRN_HEADS, HGRN_DIM)
    return (o * gate).reshape(B, S, HALF).astype(g.dtype)

def forgetting_attention(q, k, v, f_logit, b_f):
    B, S, _ = q.shape
    q = q.reshape(B, S, FOX_HEADS, FOX_DIM)
    k = k.reshape(B, S, FOX_HEADS, FOX_DIM)
    v = v.reshape(B, S, FOX_HEADS, FOX_DIM)
    log_f = jax.nn.log_sigmoid(f_logit.astype(jnp.float32) + b_f.astype(jnp.float32))
    c = jnp.cumsum(log_f, axis=1).transpose(0, 2, 1)
    scale = FOX_DIM ** -0.5
    outs = []
    for blk in range(S // Q_BLOCK):
        q0, q1 = blk * Q_BLOCK, (blk + 1) * Q_BLOCK
        logits = jnp.einsum('bqhd,bkhd->bhqk', q[:, q0:q1], k[:, :q1]).astype(jnp.float32) * scale
        logits = logits + c[:, :, q0:q1, None] - c[:, :, None, :q1]
        qpos = jnp.arange(q0, q1)[:, None]
        kpos = jnp.arange(q1)[None, :]
        logits = jnp.where(kpos <= qpos, logits, -jnp.inf)
        p = jax.nn.softmax(logits, axis=-1)
        outs.append(jnp.einsum('bhqk,bkhd->bqhd', p.astype(v.dtype), v[:, :q1]))
    return jnp.concatenate(outs, axis=1).reshape(B, S, HALF)

def stick_breaking_attention(q, k, v):
    B, S, _ = q.shape
    q = q.reshape(B, S, SB_HEADS, SB_DIM)
    k = k.reshape(B, S, SB_HEADS, SB_DIM)
    v = v.reshape(B, S, SB_HEADS, SB_DIM)
    scale = SB_DIM ** -0.5
    outs = []
    for blk in range(S // Q_BLOCK):
        q0, q1 = blk * Q_BLOCK, (blk + 1) * Q_BLOCK
        z = jnp.einsum('bqhd,bkhd->bhqk', q[:, q0:q1], k[:, :q1]).astype(jnp.float32) * scale
        qpos = jnp.arange(q0, q1)[:, None]
        kpos = jnp.arange(q1)[None, :]
        mask = kpos < qpos
        log_one_minus = jnp.where(mask, jax.nn.log_sigmoid(-z), 0.0)
        suffix = lax.cumsum(log_one_minus, axis=3, reverse=True) - log_one_minus
        log_w = jax.nn.log_sigmoid(z) + suffix
        w = jnp.where(mask, jnp.exp(log_w), 0.0)
        outs.append(jnp.einsum('bhqk,bkhd->bqhd', w.astype(v.dtype), v[:, :q1]))
    return jnp.concatenate(outs, axis=1).reshape(B, S, HALF)

def rg_lru_branch(xr, gate, conv_w, conv_b, wa, ba, wx, bx, lam):
    B, S, W = xr.shape
    xpad = jnp.pad(xr, ((0, 0), (CONV_WIDTH - 1, 0), (0, 0)))
    xc = conv_b + sum(conv_w[j] * xpad[:, j:j + S] for j in range(CONV_WIDTH))
    xb = xc.reshape(B, S, LRU_BLOCKS, LRU_BLOCK_DIM)
    r = jax.nn.sigmoid(jnp.einsum('bsni,nij->bsnj', xb, wa).reshape(B, S, W) + ba)
    i = jax.nn.sigmoid(jnp.einsum('bsni,nij->bsnj', xb, wx).reshape(B, S, W) + bx)
    log_a = -LRU_C * r.astype(jnp.float32) * jax.nn.softplus(-lam.astype(jnp.float32))
    a = jnp.exp(log_a)
    u = jnp.sqrt(-jnp.expm1(2.0 * log_a)) * (i * xc).astype(jnp.float32)

    def combine(left, right):
        a1, b1 = left
        a2, b2 = right
        return a1 * a2, a2 * b1 + b2

    _, h = lax.associative_scan(combine, (a, u), axis=1)
    return (h * jax.nn.gelu(gate.astype(jnp.float32), approximate=True)).astype(xr.dtype)

def swiglu_2(x, w13, w2):
    a, b = jnp.split(x @ w13, 2, axis=-1)
    return (jax.nn.silu(a) * b) @ w2

def second_inputs(seed: int = 0) -> dict:
    key = jax.random.key(seed)
    ks = jax.random.split(key, 24)
    f32 = jnp.float32
    nrm = lambda k, shp, s: jax.random.normal(k, shp, f32) * s
    x = jax.random.normal(ks[0], (BATCH, SEQ, D_MODEL), f32)
    ev_w_in = nrm(ks[1], (N_EVEN_2, D_MODEL, EVEN_IN_2), D_MODEL ** -0.5)
    ev_fox_bf = 1.0 + nrm(ks[2], (N_EVEN_2, FOX_HEADS), 0.1)
    hgrn_lb = nrm(ks[3], (DEPTH + 1, HALF), 0.1)
    ev_hgrn_norm_g = 1.0 + nrm(ks[4], (N_EVEN_2, HGRN_DIM), 0.02)
    ev_w_out = nrm(ks[5], (N_EVEN_2, D_MODEL, D_MODEL), BETA * D_MODEL ** -0.5)
    od_w_in = nrm(ks[6], (N_ODD_2, D_MODEL, ODD_IN), D_MODEL ** -0.5)
    od_conv_w = nrm(ks[7], (N_ODD_2, CONV_WIDTH, LRU_WIDTH), CONV_WIDTH ** -0.5)
    od_conv_b = nrm(ks[8], (N_ODD_2, LRU_WIDTH), 0.02)
    od_gate_a_w = nrm(ks[9], (N_ODD_2, LRU_BLOCKS, LRU_BLOCK_DIM, LRU_BLOCK_DIM), LRU_BLOCK_DIM ** -0.5)
    od_gate_a_b = nrm(ks[10], (N_ODD_2, LRU_WIDTH), 0.02)
    od_gate_x_w = nrm(ks[11], (N_ODD_2, LRU_BLOCKS, LRU_BLOCK_DIM, LRU_BLOCK_DIM), LRU_BLOCK_DIM ** -0.5)
    od_gate_x_b = nrm(ks[12], (N_ODD_2, LRU_WIDTH), 0.02)
    a_c = jax.random.uniform(ks[13], (N_ODD_2, LRU_WIDTH), f32, 0.9, 0.999) ** (1.0 / LRU_C)
    od_lru_lambda = jnp.log(a_c) - jnp.log1p(-a_c)
    od_w_out = nrm(ks[14], (N_ODD_2, D_MODEL, D_MODEL), BETA * D_MODEL ** -0.5)
    ffn_w13 = nrm(ks[15], (DEPTH, D_MODEL, 2 * D_FF), D_MODEL ** -0.5)
    ffn_w2 = nrm(ks[16], (DEPTH, D_FF, D_MODEL), BETA * D_FF ** -0.5)
    ln_g = 1.0 + nrm(ks[17], (DEPTH, 2, D_MODEL), 0.02)
    ln_b = nrm(ks[18], (DEPTH, 2, D_MODEL), 0.02)
    return {'x': x, 'ev_w_in': ev_w_in, 'ev_fox_bf': ev_fox_bf, 'hgrn_lb': hgrn_lb,
            'ev_hgrn_norm_g': ev_hgrn_norm_g, 'ev_w_out': ev_w_out, 'od_w_in': od_w_in,
            'od_conv_w': od_conv_w, 'od_conv_b': od_conv_b, 'od_gate_a_w': od_gate_a_w,
            'od_gate_a_b': od_gate_a_b, 'od_gate_x_w': od_gate_x_w, 'od_gate_x_b': od_gate_x_b,
            'od_lru_lambda': od_lru_lambda, 'od_w_out': od_w_out, 'ffn_w13': ffn_w13,
            'ffn_w2': ffn_w2, 'ln_g': ln_g, 'ln_b': ln_b}

def second_block(x, ev_w_in, ev_fox_bf, hgrn_lb, ev_hgrn_norm_g, ev_w_out, od_w_in, od_conv_w,
              od_conv_b, od_gate_a_w, od_gate_a_b, od_gate_x_w, od_gate_x_b, od_lru_lambda,
              od_w_out, ffn_w13, ffn_w2, ln_g, ln_b):
    lb_all = jnp.cumsum(jax.nn.softmax(hgrn_lb.astype(jnp.float32), axis=0), axis=0)
    for layer in range(DEPTH):
        if layer % 2 == 0:
            e = layer // 2
            proj = x @ ev_w_in[e]
            qa, fa, ia, ga, qb, kb, vb, fb = split_cols_2(proj, [HALF] * 7 + [FOX_HEADS])
            ya = hgrn2(qa, fa, ia, ga, lb_all[layer], ev_hgrn_norm_g[e])
            yb = forgetting_attention(qb, kb, vb, fb, ev_fox_bf[e])
            mix = jnp.concatenate([ya, yb], axis=-1) @ ev_w_out[e]
        else:
            o = layer // 2
            proj = x @ od_w_in[o]
            xr, gr, qd, kd, vd = split_cols_2(proj, [LRU_WIDTH, LRU_WIDTH, HALF, HALF, HALF])
            yc = rg_lru_branch(xr, gr, od_conv_w[o], od_conv_b[o], od_gate_a_w[o], od_gate_a_b[o],
                               od_gate_x_w[o], od_gate_x_b[o], od_lru_lambda[o])
            yd = stick_breaking_attention(qd, kd, vd)
            mix = jnp.concatenate([yc, yd], axis=-1) @ od_w_out[o]
        x = layer_norm_2(ALPHA * x + mix, ln_g[layer, 0], ln_b[layer, 0])
        x = layer_norm_2(ALPHA * x + swiglu_2(x, ffn_w13[layer], ffn_w2[layer]), ln_g[layer, 1], ln_b[layer, 1])
    return x


def setup_inputs(seed=0):
    out = dict(first_inputs(seed))
    for name, value in second_inputs(seed + 1).items():
        if name != "x":
            out[name + "_2"] = value
    return out


def reference(
    x, mem, even_w_in, even_gate_b, even_conv_w, even_rpb, even_w_out, odd_w_in, odd_lambda,
    odd_subln_g, odd_w_out, mem_wq, mem_wkv, mem_wo, ffn_w_gu, ffn_w_down, ln_g, ln_b,
    ev_w_in_2, ev_fox_bf_2, hgrn_lb_2, ev_hgrn_norm_g_2, ev_w_out_2, od_w_in_2, od_conv_w_2,
    od_conv_b_2, od_gate_a_w_2, od_gate_a_b_2, od_gate_x_w_2, od_gate_x_b_2, od_lru_lambda_2,
    od_w_out_2, ffn_w13_2, ffn_w2_2, ln_g_2, ln_b_2,
):
    x = first_block(
        x, mem, even_w_in, even_gate_b, even_conv_w, even_rpb, even_w_out, odd_w_in, odd_lambda,
        odd_subln_g, odd_w_out, mem_wq, mem_wkv, mem_wo, ffn_w_gu, ffn_w_down, ln_g, ln_b,
    )
    return second_block(
        x, ev_w_in_2, ev_fox_bf_2, hgrn_lb_2, ev_hgrn_norm_g_2, ev_w_out_2, od_w_in_2,
        od_conv_w_2, od_conv_b_2, od_gate_a_w_2, od_gate_a_b_2, od_gate_x_w_2, od_gate_x_b_2,
        od_lru_lambda_2, od_w_out_2, ffn_w13_2, ffn_w2_2, ln_g_2, ln_b_2,
    )


_drawn_inputs = setup_inputs


def setup_inputs(seed=0):
    import zlib

    import numpy as np

    out = dict(_drawn_inputs(seed))
    spreads = {}
    factors = {'even_rpb': 25.489,
     'odd_lambda': 8.0,
     'odd_subln_g': 8.0,
     'ev_fox_bf_2': 64.0,
     'hgrn_lb_2': 5.585,
     'ev_hgrn_norm_g_2': 33.103,
     'od_conv_b_2': 3.782,
     'od_gate_a_b_2': 63.76,
     'od_gate_x_b_2': 22.004}
    for name, (base, spread) in spreads.items():
        noise = np.random.default_rng([zlib.crc32(name.encode()), seed]).standard_normal(out[name].shape)
        drawn = base * np.exp(spread * noise) if base else spread * noise
        out[name] = __import__('jax').numpy.asarray(drawn.astype(out[name].dtype))
    for name, factor in factors.items():
        out[name] = (out[name] * factor).astype(out[name].dtype)
    return out
```

```python
from contextlib import ExitStack

import numpy as np
import concourse.bass as bass
from concourse import mybir

F32 = mybir.dt.float32
F32R = mybir.dt.float32r
ALU = mybir.AluOpType
ACT = mybir.ActivationFunctionType
AX_X = mybir.AxisListType.X

P = 128
D = 1024
S = 512
NT = S // P
KD = D // P
MEM = 256
MT = MEM // P
FF = 2816
NF = FF // P
NEG = -1e30
EPS = 1e-5
ALPHA = 4.0 ** 0.25
PANEL = 2048
LAM_INIT = 0.8 - 0.6 * float(np.exp(-0.3))

PAR = {}
_at = 0
for _name, _n in (("ident", 128), ("ge", 128), ("le", 128), ("strict", 128), ("gate_b", 16), ("conv_w", 40),
                  ("subln_g", 128), ("lam", 256), ("fox_b", 8), ("hgrn_lb", 12), ("norm_g", 128),
                  ("lru_w", 16), ("lru_b", 4), ("lru_ba", 4), ("lru_bx", 4), ("lru_lam", 4), ("half", 2)):
    PAR[_name] = (_at, _n)
    _at += _n
NPAR = _at


def build(nc, a, out, stages):
    with ExitStack() as ctx:
        sems = {}

        def sem(name):
            sems[name] = ctx.enter_context(nc.semaphore(name))
            return sems[name]

        BASE = 16512
        at = {"x_row": BASE}
        at["X"] = at["x_row"] + 4 * NT * D
        at["W"] = at["X"] + 2 * 4 * KD * S
        at["raw"] = at["W"] + 98304
        at["hi"] = at["raw"] + 2 * 4 * PANEL
        at["lo"] = at["hi"] + 2 * 4 * PANEL
        at["lnrow"] = at["lo"] + 2 * 4 * PANEL
        at["par"] = at["lnrow"] + 2 * 4 * D
        at["small"] = (at["par"] + 4 * NPAR + 31) // 32 * 32
        END = 229344

        def place(name, region, off, shape, dt=F32):
            size = 4
            for n in shape[1:]:
                size *= n
            start = at[region] + off
            limit = {"X": at["W"], "W": at["raw"], "small": END}.get(region, END)
            assert start + size <= limit, (name, start + size - limit)
            return nc.alloc_sbuf_tensor_at(name, shape, dt, offset=start)

        class Area:

            def __init__(self, region, off=0):
                self.region, self.off = region, off

            def __call__(self, name, shape, dt=F32):
                t = place(name, self.region, self.off, shape, dt)
                size = 4
                for n in shape[1:]:
                    size *= n
                self.off += (size + 31) // 32 * 32
                return t

        x_row = place("x_row", "x_row", 0, [P, NT, D])
        xT_hi = place("xT_hi", "X", 0, [P, KD, S], F32R)
        xT_lo = place("xT_lo", "X", 4 * KD * S, [P, KD, S], F32R)
        raw = [place(f"raw{i}", "raw", 4 * PANEL * i, [P, PANEL]) for i in range(2)]
        whi = [place(f"whi{i}", "hi", 4 * PANEL * i, [P, PANEL], F32R) for i in range(2)]
        wlo = [place(f"wlo{i}", "lo", 4 * PANEL * i, [P, PANEL], F32R) for i in range(2)]
        ln_gb = place("ln_gb", "lnrow", 0, [P, 2, D])
        par = place("par", "par", 0, [P, NPAR])
        small = Area("small")
        stats = small("stats", [P, 12])
        mv = small("mv", [P, NT, 2])
        std = small("std", [P, NT])
        rstd = small("rstd", [P, NT])
        nmx = small("nmx", [P, 64])
        mxs = small("mxs", [P, 64])
        rsum = small("rsum", [P, 64])
        rec = small("rec", [P, 64])
        scol = small("scol", [P, 64])
        eps_col = small("eps_col", [P, 1])
        one_col = small("one_col", [P, 1])
        PS = ctx.enter_context(nc.psum_tensor("PS", [P, 8, 512], F32))

        def pcol(name, i=0, n=None):
            o, w = PAR[name]
            return par[:, o + i:o + (w if n is None else i + n)]

        ident = pcol("ident")

        w = Area("W")
        h_hi = w("h_hi", [P, NF, S], F32R)
        h_lo = w("h_lo", [P, NF, S], F32R)
        sil = w("sil", [P, 2, S])
        htmp = w("htmp", [P, 2, S])
        w = Area("W")
        mem_row = w("mem_row", [P, MT, D])
        memT_hi = w("memT_hi", [P, KD, MEM], F32R)
        memT_lo = w("memT_lo", [P, KD, MEM], F32R)
        c_kT = w("c_kT", [P, KD, MEM])
        c_v = w("c_v", [P, MT, D])
        c_qT = w("c_qT", [P, KD, S])
        c_row = w("c_row", [P, NT, D])
        c_p = w("c_p", [P, 3, MEM])
        c_pt = w("c_pt", [P, 2, MEM])
        w = Area("W")
        a_qk = w("a_qk", [P, 8, S])
        a_v = w("a_v", [P, NT, 4, 129])
        a_o = w("a_o", [P, NT, 512])
        b_qT = w("b_qT", [P, 8, S])
        b_kT = w("b_kT", [P, 4, S])
        b_v = w("b_v", [P, NT, 512])
        a_row = w("a_row", [P, NT, D])
        wg = w("wg", [P, 8, 16])
        wg_hi = w("wg_hi", [P, 8, 16], F32R)
        wg_lo = w("wg_lo", [P, 8, 16], F32R)
        gcol = w("gcol", [P, NT, 16])
        gtmp = w("gtmp", [P, 2, NT, 8])
        mcol = w("mcol", [P, 3, 2, NT, 4])
        winmask = w("winmask", [P, 64])
        pre_at = w.off
        a_pre = w("a_pre", [P, 2, S + 4])
        w = Area("W", pre_at)
        rtab = w("rtab", [P, 2, 16, 64])
        w = Area("X")
        rows = w("rows", [P, 8, S])
        m_mrow = w("m_mrow", [P, 2, 8])
        m_state = w("m_state", [P, NT, 129])
        mtmp = w("mtmp", [P, S])
        m_e = w("m_e", [P, S])
        m_qs = w("m_qs", [P, S])
        m_kp = w("m_kp", [P, S])
        w = Area("X")
        n_add = w("n_add", [P, 2, 512])
        n_p = w("n_p", [P, 3, 512])
        n_pt = w("n_pt", [P, 2, 512])
        w = Area("W")
        d_qT = w("d_qT", [P, 16, S])
        d_kT = w("d_kT", [P, 8, S])
        d_v = w("d_v", [P, NT, D])
        d_row = w("d_row", [P, NT, D])
        d_cs = w("d_cs", [P, 2, S])
        d_xs = w("d_xs", [P, 2, S])
        d_tmp = w("d_tmp", [P, 2, S])
        lam_tmp = d_tmp[:, 0, 0:128].rearrange("p (a d) -> p a d", a=2)
        d_swap = w("d_swap", [P, P])
        w = Area("X")
        d_p = w("d_p", [P, 3, 2, 512])
        d_a = w("d_a", [P, 3, 512])
        d_pt = w("d_pt", [P, 2, 512])
        d_sq = w("d_sq", [P, 512])
        w = Area("W")
        g_qT = w("g_qT", [P, 4, S])
        g_kT = w("g_kT", [P, 4, S])
        g_b = w("g_b", [P, 4, S])
        g_v = w("g_v", [P, NT, 512])
        g_g = w("g_g", [P, NT, 512])
        f_qT = w("f_qT", [P, 8, S])
        f_kT = w("f_kT", [P, 4, S])
        f_v = w("f_v", [P, NT, 512])
        g_row = w("g_row", [P, NT, D])
        g_lev = w("g_lev", [P, 8, P])
        f_w = w("f_w", [P, 8, 8])
        f_whi = w("f_whi", [P, 8, 8], F32R)
        f_wlo = w("f_wlo", [P, 8, 8], F32R)
        f_col = w("f_col", [P, NT, 8])
        f_tmp = w("f_tmp", [P, 2, NT, 8])
        w = Area("X")
        g_rst = w("g_rst", [P, S])
        g_d2 = w("g_d2", [P, 2, S])
        g_e = w("g_e", [P, 2, S])
        g_qe = w("g_qe", [P, 2, S])
        g_ke = w("g_ke", [P, 2, S])
        g_s = w("g_s", [P, 2, S])
        g_kh = w("g_kh", [P, S])
        g_khr = w("g_khr", [P, S])
        g_qh = w("g_qh", [P, S])
        g_state = w("g_state", [P, NT, P])
        w = Area("X")
        f_c = w("f_c", [P, 8, S])
        f_add = w("f_add", [P, 2, 512])
        f_p = w("f_p", [P, 3, 512])
        f_pt = w("f_pt", [P, 2, 512])
        f_rows = place("f_rows", "X", 8192 * 2 + 4096 + 1024, [P, S])
        g_e4 = place("g_e4", "X", 0, [P, NT, 512])
        f_zero = place("f_zero", "X", 8192 * 2 + 4096 + 1024 + 2048, [P, S])
        w = Area("W")
        s_qT = w("s_qT", [P, 8, S])
        s_kT = w("s_kT", [P, 4, S])
        s_v = w("s_v", [P, NT, 512])
        s_row = w("s_row", [P, NT, 512])
        l_g = w("l_g", [P, 4, S])
        l_pre = w("l_pre", [P, 4, S + 3])
        l_xc = w("l_xc", [P, 4, S])
        l_w = w("l_w", [P, 2, 4, P])
        s_at = w.off
        l_r = w("l_r", [P, 4, S])
        l_i = w("l_i", [P, 4, S])
        l_a = place("l_a", "X", 4 * 4 * S, [P, 4, S])
        l_t = place("l_t", "X", 4 * 12 * S, [P, 4, S])
        w = Area("W", s_at - 4 * 2 * 4 * P - 4 * 4 * S)
        s_pos = w("s_pos", [P, 2, 512])
        s_neg = w("s_neg", [P, 2, 512])
        s_c = w("s_c", [P, 2, 513])
        s_p = w("s_p", [P, 3, 512])
        s_pt = w("s_pt", [P, 2, 512])
        s_mask = w("s_mask", [P, 512])

        panel_loaded = [sem(f"panel_loaded{i}") for i in range(2)]
        panel_hi = sem("panel_hi")
        panel_split = sem("panel_split")
        panel_used = sem("panel_used")
        phase = {e: sem(f"phase_{e}") for e in ("pe", "act", "dve")}
        inputs_in = sem("inputs_in")
        proj_ready = sem("proj_ready")
        evac_act = sem("evac_act")
        evac_dve = sem("evac_dve")
        act_step = sem("act_step")
        dve_step = sem("dve_step")
        act_out = sem("act_out")
        dve_out = sem("dve_out")
        y_ready = sem("y_ready")
        var_ready = sem("var_ready")
        std_ready = sem("std_ready")
        row_ready = sem("row_ready")
        turned = sem("turned")
        hi_ready = sem("hi_ready")
        lo_ready = sem("lo_ready")
        s_ready = sem("s_ready")
        stat_ready = sem("stat_ready")
        exp_done = sem("exp_done")
        p_ready = sem("p_ready")
        pt_psum = sem("pt_psum")
        pt_sb = sem("pt_sb")
        pv_done = sem("pv_done")
        o_out = sem("o_out")
        pe_step = sem("pe_step")
        stored = sem("stored")

        counts = {}

        def count(name, n=1):
            counts[name] = counts.get(name, 0) + n
            return counts[name]

        extra = {}

        def S_(name):
            if name not in extra:
                extra[name] = sem(name)
            return extra[name]

        panels = []
        panel_done = []

        def cols(wt, c0, n, k0=0, nk=KD):
            assert nk * n == PANEL
            panels.append(wt[k0 * P:(k0 + nk) * P, c0:c0 + n].rearrange("(k p) c -> p k c", p=P))

        class Job:

            def __init__(self, kind, eng, name, i):
                self.kind, self.eng, self.name, self.i = kind, eng, name, i
                self.slots = 2 if kind in ("R", "GU") else 1
                self.panels = {"T": 1, "TM": 1}.get(kind, 2)

        def t_jobs(kind, wt, c0, n, eng, name):
            jobs = []
            for i in range(n // 256):
                cols(wt, c0 + 256 * i, 256)
                jobs.append(Job(kind, eng, name, 2 * i))
            return jobs

        def r_jobs(kind, wt, c0, n, eng, name):
            jobs = []
            for i in range(n // 512):
                cols(wt, c0 + 512 * i, 512, 0, 4)
                cols(wt, c0 + 512 * i, 512, 4, 4)
                jobs.append(Job(kind, eng, name, i))
            return jobs

        def plan(jobs, nslots, owner):
            s = 0
            for j in jobs:
                if j.slots == 2 and s % nslots == nslots - 1:
                    s += 1
                j.slot = [(s + i) % nslots for i in range(j.slots)]
                j.free = sorted({owner[k] for k in j.slot if k in owner})
                j.ready = count("proj_ready")
                j.done = (j.eng, count("evac_" + j.eng))
                for _ in range(j.panels - 1):
                    panel_done.append((panel_used, count("panel_used")))
                panel_done.append((proj_ready, j.ready))
                for k in j.slot:
                    owner[k] = j.done
                s += j.slots
            return jobs

        def down(wt, nk):
            for i in range(nk // 2):
                cols(wt, 0, 1024, 2 * i, 2)

        def plan_down(nk):
            for _ in range(nk // 2 - 1):
                panel_done.append((panel_used, count("panel_used")))
            panel_done.append((y_ready, count("y_ready", NT)))

        program = []
        for st in stages:
            nslots, nk = 4, KD
            if st[0] == "even":
                W = a["even_w_in"]
                jobs = (t_jobs("T", W, 0, 1024, "act", "qk") + r_jobs("R", W, 1024, 512, "act", "v")
                        + r_jobs("R", W, 1536, 512, "act", "o") + t_jobs("T", W, 2064, 512, "act", "bq")
                        + t_jobs("T", W, 2576, 512, "dve", "bk") + r_jobs("R", W, 3088, 512, "dve", "bv"))
                dn = a["even_w_out"]
            elif st[0] == "cross":
                l = st[1]
                kv, wq = a["mem_wkv"][l], a["mem_wq"][l]
                owner = {}
                kv_jobs = plan(t_jobs("TM", kv, 0, 1024, "act", "k") + r_jobs("RM", kv, 1024, 1024, "act", "v"), 2, owner)
                jobs = t_jobs("T", wq, 0, 1024, "act", "q")
                dn = a["mem_wo"][l]
            elif st[0] == "ffn":
                up, dn = st[1]
                jobs = []
                for i in range(FF // 256):
                    cols(up, 256 * i, 256)
                    cols(up, FF + 256 * i, 256)
                    jobs.append(Job("GU", "dve", "gu", 2 * i))
                nk = NF
            elif st[0] == "odd":
                W = a["odd_w_in"]
                jobs = (t_jobs("T", W, 0, 1024, "act", "q") + t_jobs("T", W, 1024, 1024, "act", "k")
                        + r_jobs("R", W, 2048, 1024, "act", "v"))
                dn = a["odd_w_out"]
                nslots = 3
            elif st[0] == "hgrn":
                W = a["ev_w_in_2"]
                jobs = (t_jobs("T", W, 0, 512, "act", "q") + t_jobs("T", W, 512, 512, "act", "z")
                        + r_jobs("R", W, 1024, 512, "dve", "v") + r_jobs("R", W, 1536, 512, "act", "g")
                        + t_jobs("T", W, 2048, 512, "act", "fq") + t_jobs("T", W, 2560, 512, "dve", "fk")
                        + r_jobs("R", W, 3072, 512, "dve", "fv"))
                dn = a["ev_w_out_2"]
            else:
                W = a["od_w_in_2"]
                jobs = (t_jobs("T", W, 0, 512, "act", "x") + t_jobs("T", W, 512, 512, "act", "g")
                        + t_jobs("T", W, 1024, 512, "act", "q") + t_jobs("T", W, 1536, 512, "dve", "k")
                        + r_jobs("R", W, 2048, 512, "dve", "v"))
                dn = a["od_w_out_2"]
            if st[0] == "cross":
                jobs = kv_jobs + plan(jobs, nslots, owner)
            else:
                jobs = plan(jobs, nslots, {})
            program.append((st, jobs))
            down(dn, nk)
            plan_down(nk)

        n_phase = {"pe": [0], "act": [0], "dve": [0]}

        def phase_end(eng, me):
            n_phase[me][0] += 1
            eng.drain().then_inc(phase[me], 1)
            for other in ("pe", "act", "dve"):
                if other != me:
                    eng.wait_ge(phase[other], n_phase[me][0])

        def stepper(eng, s):
            n = [0]

            def step(ins):
                n[0] += 1
                ins.then_inc(s, 1)
                eng.wait_ge(s, n[0])
            return step

        used = [0]

        def next_panel(pe, n=1):
            first = used[0]
            used[0] += n
            pe.wait_ge(panel_split, used[0])
            return [(whi[k % 2], wlo[k % 2]) for k in range(first, first + n)]

        def product(pe, o, lhs, rhs, start, stop):
            pe.matmul(o, lhs[0], rhs[0], start=start, stop=False, skip_group_check=True)
            pe.matmul(o, lhs[0], rhs[1], start=False, stop=False, skip_group_check=True)
            return pe.matmul(o, lhs[1], rhs[0], start=False, stop=stop, skip_group_check=True)

        def pe_projections(pe, jobs, after=None):
            free = {"act": evac_act, "dve": evac_dve}
            for j in jobs:
                for eng, n in j.free:
                    pe.wait_ge(free[eng], n)
                if j.kind in ("T", "TM"):
                    xh, xl, n = (xT_hi, xT_lo, S) if j.kind == "T" else (memT_hi, memT_lo, MEM)
                    (h, lo), = next_panel(pe)
                    for c in range(2):
                        o = PS[:, 2 * j.slot[0] + c, 0:n]
                        for k in range(KD):
                            sl = slice(256 * k + 128 * c, 256 * k + 128 * c + 128)
                            m = product(pe, o, (h[:, sl], lo[:, sl]), (xh[:, k, :], xl[:, k, :]), k == 0, k == KD - 1)
                    m.then_inc(proj_ready, 1)
                elif j.kind in ("R", "RM"):
                    xh, xl, n = (xT_hi, xT_lo, NT) if j.kind == "R" else (memT_hi, memT_lo, MT)
                    for half in range(2):
                        (h, lo), = next_panel(pe)
                        for t in range(n):
                            o = PS[:, 2 * j.slot[0] + t, :]
                            ts = slice(128 * t, 128 * t + 128)
                            for k in range(4):
                                kk = 4 * half + k
                                cs = slice(512 * k, 512 * k + 512)
                                m = product(pe, o, (xh[:, kk, ts], xl[:, kk, ts]), (h[:, cs], lo[:, cs]),
                                            kk == 0, kk == KD - 1)
                        m.then_inc(panel_used if half == 0 else proj_ready, 1)
                else:
                    for part in range(2):
                        (h, lo), = next_panel(pe)
                        for c in range(2):
                            o = PS[:, 2 * j.slot[part] + c, :]
                            for k in range(KD):
                                sl = slice(256 * k + 128 * c, 256 * k + 128 * c + 128)
                                m = product(pe, o, (h[:, sl], lo[:, sl]), (xT_hi[:, k, :], xT_lo[:, k, :]),
                                            k == 0, k == KD - 1)
                        m.then_inc(panel_used if part == 0 else proj_ready, 1)
                if after:
                    after(j)

        held = []

        def pe_split(pe, jobs, half, turns=None):
            if jobs[0].kind == "GU":
                parts = [(jobs[0].slot[0], panel_used), (jobs[0].slot[1], proj_ready)]
            else:
                parts = [(jobs[0].slot[0], proj_ready), (jobs[1].slot[0], proj_ready)]
            pe.wait_ge(lo_ready, n_turn["pe"])
            tok = slice(256 * half, 256 * half + 256)
            for i, (slot, done) in enumerate(parts):
                if half == 0:
                    held.extend(next_panel(pe))
                h, lo = held[i]
                for c in range(2):
                    if turns and (i, c) == (1, 1):
                        turns()
                    for k in range(KD):
                        sl = slice(256 * k + 128 * c, 256 * k + 128 * c + 128)
                        m = product(pe, PS[:, 2 * slot + c, tok], (h[:, sl], lo[:, sl]), (xT_hi[:, k, tok], xT_lo[:, k, tok]),
                                    k == 0, k == KD - 1)
                if half == 1:
                    m.then_inc(done, 1)
            if half == 1:
                held.clear()

        def rest(jobs):
            return jobs[1:] if jobs[0].kind == "GU" else jobs[2:]

        n_turn = {"pe": 0, "act": 0, "dve": 0}

        def pe_turn(pe, src, blocks, bank, wait_rows=None):
            n_turn["pe"] += 1
            if wait_rows is not None:
                pe.wait_ge(row_ready, wait_rows)
            for b in range(blocks):
                m = pe.transpose(PS[:, bank + b // 4, 128 * (b % 4):128 * (b % 4) + 128],
                                 src[:, 128 * b:128 * b + 128], ident)
            m.then_inc(turned, 1)

        def act_turn(act, dst_hi, k0, blocks, bank, t):
            n_turn["act"] += 1
            act.wait_ge(turned, n_turn["act"])
            for b in range(0, blocks, 4):
                m = act.activation(dst_hi[:, k0 + b:k0 + b + 4, 128 * t:128 * t + 128],
                                   PS[:, bank + b // 4, :].rearrange("p (k c) -> p k c", k=4), ACT.Copy)
            m.then_inc(hi_ready, 1)

        def dve_turn(dve, dst_hi, dst_lo, k0, blocks, bank, t):
            n_turn["dve"] += 1
            dve.wait_ge(turned, n_turn["dve"])
            dve.wait_ge(hi_ready, n_turn["dve"])
            for b in range(0, blocks, 4):
                m = dve.tensor_tensor(dst_lo[:, k0 + b:k0 + b + 4, 128 * t:128 * t + 128],
                                      PS[:, bank + b // 4, :].rearrange("p (k c) -> p k c", k=4),
                                      dst_hi[:, k0 + b:k0 + b + 4, 128 * t:128 * t + 128].bitcast(F32), ALU.subtract)
            m.then_inc(lo_ready, 1)

        n_ln = {"pe": 0, "act": 0, "dve": 0}

        def pe_block_out(pe, order, lh, ll, nk, head):
            base = n_ln["pe"]
            n_ln["pe"] += NT

            def turn(t):
                pe_turn(pe, x_row[:, t, :], KD, 2 * t, base + t + 1)
            for i in range(nk // 2 - 2):
                (h, lo), = next_panel(pe)
                for t, was_read, n in order:
                    if i == 0:
                        pe.wait_ge(was_read, n)
                    ts = slice(128 * t, 128 * t + 128)
                    for c in range(2):
                        for k in range(2):
                            cs = slice(1024 * k + 512 * c, 1024 * k + 512 * c + 512)
                            m = product(pe, PS[:, 2 * t + c, :], (lh[:, 2 * i + k, ts], ll[:, 2 * i + k, ts]),
                                        (h[:, cs], lo[:, cs]), i == 0 and k == 0, False)
                m.then_inc(panel_used, 1)

            def add(i, t):
                ts = slice(128 * t, 128 * t + 128)
                h, lo = two[i]
                for c in range(2):
                    for k in range(2):
                        cs = slice(1024 * k + 512 * c, 1024 * k + 512 * c + 512)
                        kk = nk - 4 + 2 * i + k
                        m = product(pe, PS[:, 2 * t + c, :], (lh[:, kk, ts], ll[:, kk, ts]),
                                    (h[:, cs], lo[:, cs]), False, i == 1 and k == 1)
                return m

            def finish(t):
                add(1, t).then_inc(y_ready, 1)
            two = next_panel(pe)
            for t in (0, 1, 2):
                add(0, t)
            two += next_panel(pe)
            finish(0)
            finish(1)
            if head:
                turn(0)
            add(0, 3).then_inc(panel_used, 1)
            finish(2)
            if head:
                turn(1)
            finish(3)
            if head:
                head(pe, lambda: (turn(2), turn(3)))

        def act_block_out(act, head):
            base = n_ln["act"]
            n_ln["act"] += NT

            def square_root(t):
                act.wait_ge(var_ready, base + t + 1)
                act.activation(std[:, t:t + 1], mv[:, t, 1:2], ACT.Sqrt, bias=eps_col[:, 0:1]).then_inc(std_ready, 1)

            for t in (0, 2):
                square_root(t)
                square_root(t + 1)
                if head and t == 0:
                    act_turn(act, xT_hi, 0, KD, 0, 0)
                    act_turn(act, xT_hi, 0, KD, 2, 1)
            if head:
                head(act, lambda: (act_turn(act, xT_hi, 0, KD, 4, 2), act_turn(act, xT_hi, 0, KD, 6, 3)))
            else:
                for t in range(NT):
                    act.wait_ge(row_ready, base + t + 1)
                    act.dma_start(out[128 * t:128 * t + 128, :], x_row[:, t, :]).then_inc(stored, 16)
                act.wait_ge(stored, 16 * NT)

        def dve_block_out(dve, step, head, ln_loaded):
            base = n_ln["dve"]
            n_ln["dve"] += NT
            dve.wait_ge(*ln_loaded)
            for t in range(NT):
                dve.wait_ge(y_ready, base + t + 1)
                xt = x_row[:, t, :]
                step(dve.scalar_tensor_tensor(out=xt, in0=xt, scalar=ALPHA,
                                              in1=PS[:, 2 * t:2 * t + 2, :].rearrange("p a b -> p (a b)"),
                                              op0=ALU.mult, op1=ALU.add))
                dve.bn_stats(stats[:, 0:6], xt[:, 0:512])
                step(dve.bn_stats(stats[:, 6:12], xt[:, 512:1024]))
                m = dve.bn_aggr(mv[:, t, :], stats[:, 0:12])
                m.then_inc(var_ready, 1)
                dve.wait_ge(var_ready, base + t + 1)
                step(dve.scalar_tensor_tensor(out=xt, in0=xt, scalar=mv[:, t, 0:1], in1=ln_gb[:, 0, :],
                                              op0=ALU.subtract, op1=ALU.mult))
                dve.wait_ge(std_ready, base + t + 1)
                step(dve.reciprocal(rstd[:, t:t + 1], std[:, t:t + 1]))
                dve.scalar_tensor_tensor(out=xt, in0=xt, scalar=rstd[:, t:t + 1], in1=ln_gb[:, 1, :],
                                         op0=ALU.mult, op1=ALU.add).then_inc(row_ready, 1)
                if head and t == 1:
                    dve_turn(dve, xT_hi, xT_lo, 0, KD, 0, 0)
                    dve_turn(dve, xT_hi, xT_lo, 0, KD, 2, 1)
            if head:
                head(dve, lambda: (dve_turn(dve, xT_hi, xT_lo, 0, KD, 4, 2), dve_turn(dve, xT_hi, xT_lo, 0, KD, 6, 3)))

        def pe_rows(pe, row, k0, blocks):
            for t in range(NT):
                pe_turn(pe, row[:, t, :], blocks, 2 * t)

        def act_rows(act, k0, blocks):
            for t in range(NT):
                act_turn(act, xT_hi, k0, blocks, 2 * t, t)

        def dve_rows(dve, k0, blocks):
            for t in range(NT):
                dve_turn(dve, xT_hi, xT_lo, k0, blocks, 2 * t, t)

        def load_next(act):
            if at_stage[0] + 1 < len(code):
                code[at_stage[0] + 1]["act_load"](act)

        at_stage = [0]
        loads = {}

        def load(act, name, dst, src):
            s = name.rstrip("0123456789") + "_loaded"
            loads[name] = (S_(s), count(s, 16))
            act.dma_start(dst, src).then_inc(S_(s), 16)

        def evacuations(eng, me, jobs, f):
            done = {"act": evac_act, "dve": evac_dve}[me]
            for j in jobs:
                if j.eng == me:
                    eng.wait_ge(proj_ready, j.ready)
                    f(j).then_inc(done, 1)

        class Units:
            lag = 2

            def __init__(self, n, nk, s_banks, pt_banks, o_banks, group, s_free, p, pt, last_of):
                self.n, self.nk, self.s_banks, self.pt_banks, self.o_banks = n, nk, s_banks, pt_banks, o_banks
                self.group, self.s_free, self.p, self.pt, self.last_of = group, s_free, p, pt, last_of
                self.u0 = counts.get("units", 0)
                self.g0 = counts.get("groups", 0)
                self.groups = group(n - 1) + 1
                count("units", n)
                count("groups", self.groups)

            def ps(self, u):
                return self.s_banks[u % len(self.s_banks)]

            def ptb(self, u):
                return self.pt_banks[u % 2]

            def ob(self, u):
                return self.o_banks[self.group(u) % len(self.o_banks)]

        def pe_units(pe, A, scores, values, weights_ready):
            nS = len(A.s_banks)
            opened = set()
            for i in range(A.n + A.lag + 1):
                if i < A.n:
                    if i >= nS:
                        pe.wait_ge(A.s_free, A.u0 + i - nS + 1)
                    scores(i, A.ps(i)).then_inc(s_ready, 1)
                if A.lag <= i < A.n + A.lag:
                    u = i - A.lag
                    pe.wait_ge(*weights_ready(u))
                    if u >= 2:
                        pe.wait_ge(pt_sb, A.u0 + u - 1)
                    for k in range(A.nk(u)):
                        m = pe.transpose(PS[:, A.ptb(u), 128 * k:128 * k + 128], A.p(u)[:, 128 * k:128 * k + 128], ident)
                    m.then_inc(pt_psum, 1)
                if i > A.lag:
                    u = i - A.lag - 1
                    pe.wait_ge(pt_sb, A.u0 + u + 1)
                    g = A.group(u)
                    if g not in opened:
                        opened.add(g)
                        if g >= len(A.o_banks):
                            pe.wait_ge(o_out, A.g0 + g - len(A.o_banks) + 1)
                    c0, dv = values(u, 0)[1:]
                    for k in range(A.nk(u)):
                        v = values(u, k)[0]
                        m = pe.matmul(PS[:, A.ob(u), c0:c0 + dv], A.pt(u)[:, 128 * k:128 * k + 128], v,
                                      start=k == 0, stop=k == A.nk(u) - 1, skip_group_check=True)
                    m.then_inc(pv_done, 1)

        def act_units(act, A, exps):
            for i in range(A.n + A.lag):
                if i >= A.lag:
                    u = i - A.lag
                    act.wait_ge(pt_psum, A.u0 + u + 1)
                    if u >= 2:
                        act.wait_ge(pv_done, A.u0 + u - 1)
                    w = 128 * A.nk(u)
                    act.activation(A.pt(u)[:, 0:w], PS[:, A.ptb(u), 0:w], ACT.Copy).then_inc(pt_sb, 1)
                if i < A.n:
                    exps(i)

        def dve_units(dve, A, stats_, store):
            todo = []
            behind = A.lag + 1
            for i in range(A.n + behind + 1):
                if i < A.n:
                    stats_(i)
                    if A.last_of(i):
                        todo.append((i, A.group(i)))
                while todo and (todo[0][0] + behind <= i or i >= A.n):
                    u, g = todo.pop(0)
                    dve.wait_ge(pv_done, A.u0 + u + 1)
                    store(g, A.ob(u)).then_inc(o_out, 1)

        def softmax_exp(act, A, u, src, scale, width, p):
            act.wait_ge(stat_ready, A.u0 + u + 1)
            if u >= 3:
                act.wait_ge(pt_psum, A.u0 + u - 2)
            act.activation(p[:, 0:width], src, ACT.Exp, bias=nmx[:, u:u + 1], scale=scale,
                           accum_out=rsum[:, u:u + 1]).then_inc(exp_done, 1)

        stage_no = {"cross": 0, "ffn": 0}

        def stage_cross(st, jobs):
            l = st[1]
            mem = a["mem"]
            A = Units(NT * 4, lambda u: MT, [0, 1, 2, 3], [4, 5], [6, 7], lambda u: u // 2, exp_done,
                      lambda u: c_p[:, u % 3, :], lambda u: c_pt[:, u % 2, :], lambda u: u % 2 == 1)

            def act_load(act):
                load(act, f"mem{l}", mem_row[:, :, :], mem.rearrange("(t p) d -> p t d", p=P))

            nk_ = len(jobs) - 4
            early, late, q_jobs = jobs[0:nk_ - 3], jobs[nk_ - 3:nk_], jobs[nk_:]

            def memory_pe(pe):
                pe.wait_ge(*loads[f"mem{l}"])
                first = n_turn["pe"] - NT
                for t in range(MT):
                    pe.wait_ge(lo_ready, first + t + 1)
                    pe_turn(pe, mem_row[:, t, :], KD, 2 * t)

            def memory_act(act):
                for t in range(MT):
                    act_turn(act, memT_hi, 0, KD, 2 * t, t)

            def memory_dve(dve):
                for t in range(MT):
                    dve_turn(dve, memT_hi, memT_lo, 0, KD, 2 * t, t)

            def head_pe(pe, turns):
                pe.wait_ge(lo_ready, n_turn["pe"])
                pe_projections(pe, early)
                turns()

            def evac_kv(act, jobs):
                def evac(j):
                    if j.name == "k":
                        for c in range(2):
                            m = act.activation(c_kT[:, j.i + c, :], PS[:, 2 * j.slot[0] + c, 0:MEM], ACT.Copy)
                        return m
                    for t in range(MT):
                        m = act.activation(c_v[:, t, 512 * j.i:512 * j.i + 512], PS[:, 2 * j.slot[0] + t, :], ACT.Copy)
                    return m
                evacuations(act, "act", jobs, evac)

            def head_act(act, turns):
                evac_kv(act, early)
                turns()

            def act(act, step):
                evac_kv(act, late)

                def evac(j):
                    for c in range(2):
                        m = act.activation(c_qT[:, j.i + c, :], PS[:, 2 * j.slot[0] + c, :], ACT.Copy, scale=1.0 / 16)
                    return m
                evacuations(act, "act", q_jobs, evac)
                phase_end(act, "act")
                act_units(act, A, lambda u: softmax_exp(act, A, u, PS[:, A.ps(u), 0:MEM], 1.0, MEM, A.p(u)))
                phase_end(act, "act")
                act_rows(act, 0, KD)

            def dve(dve, step):
                phase_end(dve, "dve")

                def stat(u):
                    dve.wait_ge(s_ready, A.u0 + u + 1)
                    dve.tensor_reduce(nmx[:, u:u + 1], PS[:, A.ps(u), 0:MEM], AX_X, ALU.max, negate=True)\
                        .then_inc(stat_ready, 1)

                def store(g, bank):
                    step(dve.reciprocal(rec[:, 2 * g:2 * g + 2], rsum[:, 2 * g:2 * g + 2]))
                    t, hh = g // 2, g % 2
                    return dve.tensor_tensor(c_row[:, t, 512 * hh:512 * hh + 512].rearrange("p (h d) -> p h d", h=2),
                                             PS[:, bank, :].rearrange("p (h d) -> p h d", h=2),
                                             rec[:, 2 * g:2 * g + 2].unsqueeze(2).to_broadcast([P, 2, 256]), ALU.mult)
                dve_units(dve, A, stat, store)
                phase_end(dve, "dve")
                dve_rows(dve, 0, KD)

            def pe(pe):
                pe_projections(pe, late)
                pe.wait_ge(lo_ready, n_turn["pe"])
                pe_projections(pe, q_jobs)
                phase_end(pe, "pe")

                def scores(u, bank):
                    t, h = u // 4, u % 4
                    for k in range(2):
                        m = pe.matmul(PS[:, bank, 0:MEM], c_qT[:, 2 * h + k, 128 * t:128 * t + 128], c_kT[:, 2 * h + k, :],
                                      start=k == 0, stop=k == 1, skip_group_check=True)
                    return m

                def values(u, k):
                    h = u % 4
                    return c_v[:, k, 256 * h:256 * h + 256], 256 * (h % 2), 256
                pe_units(pe, A, scores, values, lambda u: (exp_done, A.u0 + u + 1))
                phase_end(pe, "pe")
                pe_rows(pe, c_row, 0, KD)
            return {"act_load": act_load, "act": act, "dve": dve, "pe": pe,
                    "memory": {"pe": memory_pe, "act": memory_act, "dve": memory_dve},
                    "head": {"pe": head_pe, "act": head_act, "dve": lambda dve, turns: turns()}}

        def stage_ffn(st, jobs):
            n0 = counts.get("ffn_tiles", 0)
            count("ffn_tiles", NF)
            sil_ready, h_ready, hhi_ready = S_("silu_ready"), S_("hidden_ready"), S_("hidden_hi_ready")

            def act(act, step):
                for j in jobs:
                    act.wait_ge(proj_ready, j.ready)
                    for c in range(2):
                        i = j.i + c
                        n = n0 + i
                        if i >= 2:
                            act.wait_ge(h_ready, n - 1)
                        act.activation(sil[:, i % 2, :], PS[:, 2 * j.slot[0] + c, :], ACT.Silu).then_inc(sil_ready, 1)
                    for c in range(2):
                        i = j.i + c
                        act.wait_ge(h_ready, n0 + i + 1)
                        act.activation(h_hi[:, i, :], htmp[:, i % 2, :], ACT.Copy).then_inc(hhi_ready, 1)

            def dve(dve, step):
                for j in jobs:
                    if j.i >= 2:
                        dve.wait_ge(evac_dve, j.done[1] - 1)
                    for c in range(2):
                        i = j.i + c
                        n = n0 + i
                        dve.wait_ge(sil_ready, n + 1)
                        m = dve.tensor_tensor(htmp[:, i % 2, :], sil[:, i % 2, :], PS[:, 2 * j.slot[1] + c, :], ALU.mult)
                        m.then_inc(h_ready, 1)
                    for c in range(2):
                        i = j.i + c
                        dve.wait_ge(h_ready, n0 + i + 1)
                        dve.wait_ge(hhi_ready, n0 + i + 1)
                        m = dve.tensor_tensor(h_lo[:, i, :], htmp[:, i % 2, :], h_hi[:, i, :].bitcast(F32), ALU.subtract)
                    m.then_inc(evac_dve, 1)

            def pe(pe):
                pe_split(pe, jobs, 1)
                pe_projections(pe, rest(jobs))
            return {"act_load": lambda act: None, "act": act, "dve": dve, "pe": pe, "lhs": (h_hi, h_lo, NF),
                    "free": sorted((owner.done[1], k) for k, owner in {k: j for j in jobs for k in j.slot}.items())}

        def stage_even(st, jobs):
            A = Units(8 * NT, lambda u: 4, [0, 1], [2, 3], [4, 5, 6, 7], lambda u: u % NT, stat_ready,
                      lambda u: n_p[:, u % 3, :], lambda u: n_pt[:, u % 2, :], lambda u: u >= 8 * NT - NT)
            A.groups = NT
            names = ["gate_sum", "gate_abs", "gate_ln", "gate_col", "gate_rows", "wg_cut", "pre_ready", "conv_ready",
                     "row_exp_in", "row_exps", "row_kinds", "cols_psum", "cols_ready", "m_kq", "m_bcast", "m_kv",
                     "m_num", "m_arg", "m_qsi", "m_st", "m_sm", "m_kps", "m_exp", "m_out", "ones_ready", "row_zero"]
            G = {n: S_(n) for n in names}
            chunk = lambda c: slice(128 * c, 128 * c + 128)

            def act_load(act):
                load(act, "gates", wg[:, :, :], a["even_w_in"][:, 2048:2064].rearrange("(k p) c -> p k c", p=P))
                load(act, "gates", winmask[:, :], a["winmask"])

            def load_table(act, h):
                act.dma_start(rtab[:, h % 2, :, :], a["rpb"][h]).then_inc(S_(f"rtab_loaded{h % 2}"), 16)

            def act(act, step):
                act.wait_ge(G["gate_abs"], 1)
                step(act.activation(gtmp[:, 0, :, :], gtmp[:, 0, :, :], ACT.Exp, scale=-1.0))
                act.activation(gtmp[:, 0, :, :], gtmp[:, 0, :, :], ACT.Ln, bias=one_col[:, 0:1]).then_inc(G["gate_ln"], 1)
                silu_due = []

                def silu():
                    i = silu_due.pop(0)
                    act.wait_ge(G["conv_ready"], i + 1)
                    act.activation(a_qk[:, i, :], a_qk[:, i, :], ACT.Silu)

                def evac(j):
                    s = j.slot[0]
                    if j.name == "qk":
                        for c in range(2):
                            i = j.i + c
                            if i >= 2:
                                act.wait_ge(G["conv_ready"], i - 1)
                            if i == 0:
                                act.wait_ge(G["ones_ready"], 1)
                            m = act.activation(a_pre[:, i % 2, 2:2 + S], PS[:, 2 * s + c, :], ACT.Copy)
                            if c == 0:
                                m.then_inc(G["pre_ready"], 1)
                            silu_due.append(i)
                        return m
                    if j.name == "v":
                        for t in range(NT):
                            m = act.activation(a_v[:, t, :, 0:128], PS[:, 2 * j.slot[t // 2] + t % 2, :]
                                               .rearrange("p (h d) -> p h d", h=4), ACT.Copy)
                        return m
                    if j.name == "o":
                        while silu_due:
                            silu()
                        for t in range(NT):
                            m = act.activation(a_o[:, t, :], PS[:, 2 * j.slot[t // 2] + t % 2, :], ACT.Sigmoid)
                        return m
                    for c in range(2):
                        for hh in range(2):
                            m = act.activation(b_qT[:, 2 * (j.i + c) + hh, :], PS[:, 2 * s + c, :], ACT.Copy,
                                               scale=pcol("half", hh, 1))
                    return m
                evacuations(act, "act", jobs, evac)
                phase_end(act, "act")
                load_table(act, 0)
                load_table(act, 1)
                act.wait_ge(G["row_exp_in"], 1)
                for r in (6, 7):
                    act.activation(rows[0:4, r, :], rows[0:4, r, :], ACT.Exp)
                for r in (2, 3):
                    act.activation(rows[0:4, r, :], rows[0:4, r, :], ACT.Exp, scale=-1.0)
                act.activation(m_e[0:4, :], m_e[0:4, :], ACT.Exp)
                act.activation(m_qs[0:4, :], m_qs[0:4, :], ACT.Exp).then_inc(G["row_exps"], 1)
                act.wait_ge(G["cols_psum"], 1)
                act.activation(mcol[:, :, :, :, :].rearrange("p a b c d -> p (a b c d)"), PS[:, 4, 0:96], ACT.Copy)\
                    .then_inc(G["cols_ready"], 1)
                act.wait_ge(G["cols_ready"], 1)
                for j in range(8):
                    h, d = j // 2, j % 2
                    act.wait_ge(G["m_kq"], h + 1)
                    if j >= 1:
                        act.wait_ge(G["m_kv"], j)
                    for c in range(NT):
                        m = act.activation(m_kp[:, chunk(c)], PS[:, 1, chunk(c)], ACT.Copy, scale=mcol[:, 2, d, c, h:h + 1])
                    m.then_inc(G["m_kps"], 1)
                    act.wait_ge(G["m_arg"], j + 1)
                    if j >= 1:
                        act.wait_ge(G["m_num"], j)
                    for c in range(NT):
                        m = act.activation(m_e[:, chunk(c)], mtmp[:, chunk(c)], ACT.Exp, bias=mcol[:, 0, d, c, h:h + 1])
                    m.then_inc(G["m_exp"], 1)
                phase_end(act, "act")

                def exps(u):
                    h = u // NT
                    if u % NT == 0 and 1 <= h < 7:
                        act.wait_ge(stat_ready, A.u0 + u)
                        load_table(act, h + 1)
                    softmax_exp(act, A, u, n_add[:, u % 2, :], -1.0, 512, A.p(u))
                act_units(act, A, exps)
                phase_end(act, "act")
                load_next(act)
                act_rows(act, 0, KD)

            def dve(dve, step):
                dve.memset(a_v[:, :, :, 128:129], 1.0)
                dve.memset(a_pre[:, :, 0:2], 0.0)
                dve.memset(a_pre[:, :, S + 2:S + 4], 0.0).then_inc(G["ones_ready"], 1)
                dve.wait_ge(*loads["gates"])
                step(dve.tensor_copy(wg_hi[:, :, :], wg[:, :, :]))
                dve.tensor_tensor(wg_lo[:, :, :], wg[:, :, :], wg_hi[:, :, :].bitcast(F32), ALU.subtract)\
                    .then_inc(G["wg_cut"], 1)
                dve.wait_ge(G["gate_sum"], 1)
                step(dve.tensor_tensor(gcol[:, :, :], PS[:, 7, 0:64].rearrange("p (t g) -> p t g", t=NT),
                                       pcol("gate_b").unsqueeze(1).to_broadcast([P, NT, 16]), ALU.add))
                dve.tensor_scalar(gtmp[:, 1, :, :], gcol[:, :, 8:16], 0.0, None, ALU.min)
                dve.scalar_tensor_tensor(out=gtmp[:, 0, :, :], in0=gcol[:, :, 8:16], scalar=-1.0, in1=gcol[:, :, 8:16],
                                         op0=ALU.mult, op1=ALU.max).then_inc(G["gate_abs"], 1)
                dve.wait_ge(G["gate_ln"], 1)
                dve.tensor_tensor(gcol[:, :, 8:16], gtmp[:, 1, :, :], gtmp[:, 0, :, :], ALU.subtract)\
                    .then_inc(G["gate_col"], 1)
                for i in range(8):
                    if i % 2 == 0:
                        dve.wait_ge(G["pre_ready"], i // 2 + 1)
                    else:
                        dve.wait_ge(evac_act, jobs[i // 2].done[1])
                    src, o = a_pre[:, i % 2, :], a_qk[:, i, :]
                    step(dve.tensor_scalar(o, src[:, 0:S], pcol("conv_w", i, 1), None, ALU.mult))
                    for k in range(1, 5):
                        m = dve.scalar_tensor_tensor(out=o, in0=src[:, k:k + S], scalar=pcol("conv_w", 8 * k + i, 1),
                                                     in1=o, op0=ALU.mult, op1=ALU.add)
                        if k < 4:
                            step(m)
                    m.then_inc(G["conv_ready"], 1)

                def evac(j):
                    if j.name == "bk":
                        for c in range(2):
                            m = dve.tensor_copy(b_kT[:, j.i + c, :], PS[:, 2 * j.slot[0] + c, :])
                        return m
                    for t in range(NT):
                        m = dve.tensor_copy(b_v[:, t, :], PS[:, 2 * j.slot[t // 2] + t % 2, :])
                    return m
                evacuations(dve, "dve", jobs, evac)
                phase_end(dve, "dve")
                dve.memset(rows[:, 4:8, :], 0.0).then_inc(G["row_zero"], 1)
                dve.tensor_scalar(a_qk[:, 4:8, :], a_qk[:, 4:8, :], float(P) ** -0.5, None, ALU.mult)
                dve.wait_ge(G["gate_rows"], 1)
                dve.wait_ge(G["row_zero"], 1)
                step(dve.tensor_copy(rows[0:4, 0:4, :], PS[0:4, 0:4, :]))
                for d in range(2):
                    rev = (lambda ap: ap) if d == 0 else (lambda ap: ap[:, ::-1])
                    first = slice(0, S, 128) if d == 0 else slice(127, S, 128)
                    A_, B_, W_, I_ = (rows[0:4, k + d, :] for k in (0, 2, 4, 6))
                    p_ = (m_e if d == 0 else m_qs)[0:4, :]
                    step(dve.memset(mtmp[0:4, :], 1.0))
                    step(dve.memset(mtmp[0:4, first], 0.0))
                    step(dve.tensor_tensor_scan(rev(B_), rev(mtmp[0:4, :]), rev(B_), 0.0, ALU.mult, ALU.add))
                    step(dve.tensor_tensor(A_, A_, B_, ALU.subtract))
                    step(dve.memset(mtmp[0:4, :], 0.0))
                    if d == 0:
                        step(dve.tensor_copy(mtmp[0:4, 128:S:128], B_[:, 127:S - 1:128]))
                    else:
                        step(dve.tensor_copy(mtmp[0:4, 127:S - 1:128], B_[:, 128:S:128]))
                    step(dve.tensor_tensor_scan(rev(W_), rev(mtmp[0:4, :]), rev(A_), NEG, ALU.add, ALU.max))
                    mi = m_mrow[0:4, d, 0:4]
                    step(dve.memset(mi, NEG))
                    if d == 0:
                        step(dve.tensor_tensor(mi[:, 1:4], B_[:, 127:S - 1:128], W_[:, 127:S - 1:128], ALU.add))
                    else:
                        step(dve.tensor_tensor(mi[:, 0:3], B_[:, 128:S:128], W_[:, 128:S:128], ALU.add))
                    v4 = lambda ap: ap.rearrange("p (c l) -> p c l", c=NT)
                    step(dve.tensor_tensor(v4(I_), mi.unsqueeze(2).to_broadcast([4, NT, 128]), v4(W_), ALU.subtract))
                    end = slice(127, S, 128) if d == 0 else slice(0, S, 128)
                    step(dve.tensor_tensor(v4(p_), v4(A_), W_[:, end].unsqueeze(2).to_broadcast([4, NT, 128]),
                                           ALU.subtract))
                    m = dve.tensor_tensor(B_, B_, W_, ALU.add)
                m.then_inc(G["row_exp_in"], 1)
                kq = PS[:, 0, :]
                for j in range(8):
                    h, d = j // 2, j % 2
                    dve.wait_ge(G["m_bcast"], j + 1)
                    if j >= 1:
                        dve.wait_ge(G["m_exp"], j)
                    mask = pcol("ge" if d == 0 else "le")
                    dve.tensor_tensor(mtmp[:, :].rearrange("p (c l) -> p c l", c=NT),
                                      mask.unsqueeze(1).to_broadcast([P, NT, 128]),
                                      PS[:, 2, :].rearrange("p (c l) -> p c l", c=NT), ALU.subtract).then_inc(G["m_arg"], 1)
                    if j >= 1:
                        dve.wait_ge(G["m_out"], j)
                    dve.tensor_tensor(m_qs[:, :], a_qk[:, h, :], PS[:, 3, :], ALU.mult).then_inc(G["m_qsi"], 1)
                    dve.wait_ge(G["m_kv"], j + 1)
                    order = [0, 1, 2, 3] if d == 0 else [3, 2, 1, 0]
                    kv = lambda c: PS[:, 4 + c // 2, 129 * (c % 2):129 * (c % 2) + 129]
                    last = {c: 128 * c + (127 if d == 0 else 0) for c in range(NT)}
                    step(dve.tensor_copy(m_state[:, order[1], :], kv(order[0])))
                    for n in (1, 2):
                        c, nx = order[n], order[n + 1]
                        m = dve.scalar_tensor_tensor(out=m_state[:, nx, :], in0=m_state[:, c, :],
                                                     scalar=PS[:, 3, last[c]:last[c] + 1], in1=kv(c),
                                                     op0=ALU.mult, op1=ALU.add)
                        if n == 1:
                            step(m)
                    m.then_inc(G["m_st"], 1)
                    dve.wait_ge(G["m_exp"], j + 1)
                    dve.tensor_tensor(m_e[:, :], m_e[:, :], kq, ALU.mult).then_inc(G["m_sm"], 1)
                    dve.wait_ge(G["m_num"], j + 1)
                    num = PS[:, 6:8, 0:258].rearrange("p b (c e) -> p b c e", c=2)
                    den = scol[:, 0:4].rearrange("p (b c) -> p b c", b=2)
                    dn = scol[:, 8:12].rearrange("p (b c) -> p b c", b=2).unsqueeze(3)
                    step(dve.tensor_copy(dn, num[:, :, :, 128:129]))
                    step(dve.scalar_tensor_tensor(out=den.unsqueeze(3), in0=dn, scalar=-1.0, in1=dn, op0=ALU.mult,
                                                  op1=ALU.max))
                    step(dve.tensor_tensor(scol[:, 0:4], scol[:, 0:4], mcol[:, 1, d, :, h], ALU.max))
                    step(dve.reciprocal(scol[:, 4:8], scol[:, 0:4]))
                    rc = scol[:, 4:8].rearrange("p (b c) -> p b c", b=2).unsqueeze(3).to_broadcast([P, 2, 2, 128])
                    dst = a_row[:, :, 128 * h:128 * h + 128]
                    if d == 0:
                        dve.tensor_tensor(dst.rearrange("p (b c) e -> p b c e", b=2), num[:, :, :, 0:128], rc, ALU.mult)\
                            .then_inc(G["m_out"], 1)
                    else:
                        step(dve.tensor_tensor(m_qs[:, :].rearrange("p (b c e) -> p b c e", b=2, c=2),
                                               num[:, :, :, 0:128], rc, ALU.mult))
                        step(dve.tensor_tensor(dst, dst, m_qs[:, :].rearrange("p (t e) -> p t e", t=NT), ALU.add))
                        dve.tensor_tensor(dst, dst, a_o[:, :, 128 * h:128 * h + 128], ALU.mult).then_inc(G["m_out"], 1)
                phase_end(dve, "dve")

                def stat(u):
                    h, t = u // NT, u % NT
                    if t == 0:
                        dve.wait_ge(S_(f"rtab_loaded{h % 2}"), 16 * (h // 2 + 1))
                        step(dve.tensor_tensor(rtab[:, h % 2, :, :], rtab[:, h % 2, :, :],
                                               winmask[:, :].unsqueeze(1).to_broadcast([P, 16, 64]), ALU.add))
                    dve.wait_ge(s_ready, A.u0 + u + 1)
                    if u >= 2:
                        dve.wait_ge(exp_done, A.u0 + u - 1)
                    dve.tensor_tensor_reduce(out=n_add[:, u % 2, :], in0=PS[:, A.ps(u), :],
                                             in1=rtab[:, h % 2, 7 - 2 * t:15 - 2 * t, :].rearrange("p a b -> p (a b)"),
                                             scale=-1.0, scalar=-NEG, op0=ALU.add, op1=ALU.min,
                                             accum_out=nmx[:, u:u + 1]).then_inc(stat_ready, 1)

                def store(g, bank):
                    step(dve.reciprocal(rec[:, 8 * g:8 * g + 8], rsum[:, g:32:4]))
                    return dve.tensor_tensor(a_row[:, g, 512:1024].rearrange("p (h d) -> p h d", h=8),
                                             PS[:, bank, :].rearrange("p (h d) -> p h d", h=8),
                                             rec[:, 8 * g:8 * g + 8].unsqueeze(2).to_broadcast([P, 8, 64]), ALU.mult)
                dve_units(dve, A, stat, store)
                phase_end(dve, "dve")
                dve_rows(dve, 0, KD)

            def pe(pe):
                pe_split(pe, jobs, 1)
                pe.wait_ge(G["wg_cut"], 1)
                for t in range(NT):
                    for k in range(KD):
                        m = product(pe, PS[:, 7, 16 * t:16 * t + 16], (xT_hi[:, k, chunk(t)], xT_lo[:, k, chunk(t)]),
                                    (wg_hi[:, k, :], wg_lo[:, k, :]), k == 0, k == KD - 1)
                m.then_inc(G["gate_sum"], 1)

                def before_last_slot():
                    pe.wait_ge(G["gate_col"], 1)
                pe_projections(pe, jobs[2:3])
                before_last_slot()
                pe_projections(pe, jobs[3:])
                phase_end(pe, "pe")
                for g in range(4):
                    for t in range(NT):
                        m = pe.transpose(PS[0:4, g, chunk(t)], gcol[:, t, 4 * g:4 * g + 4], ident)
                m.then_inc(G["gate_rows"], 1)
                pe.wait_ge(G["row_exps"], 1)
                for kind, src in enumerate(((rows[0:4, 0, :], rows[0:4, 1, :]), (rows[0:4, 2, :], rows[0:4, 3, :]),
                                            (m_e[0:4, :], m_qs[0:4, :]))):
                    for d in range(2):
                        for c in range(NT):
                            o = 4 * ((kind * 2 + d) * NT + c)
                            m = pe.transpose(PS[:, 4, o:o + 4], src[d][:, chunk(c)], ident[0:4, 0:4])
                m.then_inc(G["cols_psum"], 1)
                pe.wait_ge(G["cols_ready"], 1)
                for j in range(8):
                    h, d = j // 2, j % 2
                    if d == 0:
                        if j >= 1:
                            pe.wait_ge(G["m_sm"], j)
                            pe.wait_ge(G["m_kps"], j)
                        for c in range(NT):
                            pe.matmul(PS[:, 0, chunk(c)], a_qk[:, 4 + h, chunk(c)], a_qk[:, h, chunk(c)],
                                      start=True, stop=True, skip_group_check=True)
                        for c in range(NT):
                            m = pe.transpose(PS[:, 1, chunk(c)], a_qk[:, 4 + h, chunk(c)], ident)
                        m.then_inc(G["m_kq"], 1)
                    if j >= 1:
                        pe.wait_ge(G["m_st"], j)
                    one_hot = ident[:, h:h + 1].to_broadcast([P, P])
                    pe.matmul(PS[:, 2, :], one_hot, rows[:, 4 + d, :], start=True, stop=True, skip_group_check=True)
                    pe.matmul(PS[:, 3, :], one_hot, rows[:, 6 + d, :], start=True, stop=True, skip_group_check=True)\
                        .then_inc(G["m_bcast"], 1)
                    order = [0, 1, 2, 3] if d == 0 else [3, 2, 1, 0]
                    pe.wait_ge(G["m_kps"], j + 1)
                    for c in order[0:3]:
                        m = pe.matmul(PS[:, 4 + c // 2, 129 * (c % 2):129 * (c % 2) + 129], m_kp[:, chunk(c)],
                                      a_v[:, c, h, :], start=True, stop=True, skip_group_check=True)
                    m.then_inc(G["m_kv"], 1)
                    pe.wait_ge(G["m_qsi"], j + 1)
                    pe.wait_ge(G["m_st"], j + 1)
                    pe.wait_ge(G["m_sm"], j + 1)
                    if j >= 1:
                        pe.wait_ge(G["m_out"], j)
                    for n, c in enumerate(order):
                        o = PS[:, 6 + c // 2, 129 * (c % 2):129 * (c % 2) + 129]
                        m = pe.matmul(o, m_e[:, chunk(c)], a_v[:, c, h, :], start=True, stop=n == 0, skip_group_check=True)
                        if n > 0:
                            m = pe.matmul(o, m_qs[:, chunk(c)], m_state[:, c, :], start=False, stop=True,
                                          skip_group_check=True)
                    m.then_inc(G["m_num"], 1)
                phase_end(pe, "pe")

                def scores(u, bank):
                    h, t = u // NT, u % NT
                    return pe.matmul(PS[:, bank, :], b_qT[:, h, chunk(t)], b_kT[:, h // 2, :], start=True, stop=True,
                                     skip_group_check=True)

                def values(u, k):
                    h = u // NT
                    return b_v[:, k, 64 * h:64 * h + 64], 64 * h, 64
                pe_units(pe, A, scores, values, lambda u: (exp_done, A.u0 + u + 1))
                phase_end(pe, "pe")
                pe_rows(pe, a_row, 0, KD)
            return {"act_load": act_load, "act": act, "dve": dve, "pe": pe}

        def stage_odd(st, jobs):
            A = Units(8 * NT, lambda u: 4, [0, 2], [4, 5], [6, 7], lambda u: u // 4, exp_done,
                      lambda u: d_a[:, u % 3, :], lambda u: d_pt[:, u % 2, :], lambda u: u % 4 == 3)
            chunk = lambda c: slice(128 * c, 128 * c + 128)
            xs_ready, swapped, rope_done = S_("rope_in"), S_("rope_swapped"), S_("rope_done")
            lam_in, lam_exp, sq_in, sq_done, sd_done = (S_(n) for n in (
                "lam_sums", "lam_exp", "rms_sums", "rms_squares", "rms_root"))

            def xs_in(n):
                return (xs_ready, n // 2 + 1) if n % 2 == 0 else (evac_act, jobs[n // 2].done[1])

            def act_load(act):
                load(act, "rope", d_cs[:, :, :], a["rope"])
                load(act, "rope", d_swap[:, :], a["swap"])

            def act(act, step):
                act.wait_ge(lam_in, 1)
                act.activation(scol[:, 18:20], scol[:, 16:18], ACT.Exp).then_inc(lam_exp, 1)

                def evac(j):
                    if j.name == "v":
                        for t in range(NT):
                            m = act.activation(d_v[:, t, 512 * j.i:512 * j.i + 512], PS[:, 2 * j.slot[t // 2] + t % 2, :],
                                               ACT.Copy)
                        return m
                    for c in range(2):
                        n = j.i + c + (8 if j.name == "k" else 0)
                        if n >= 2:
                            act.wait_ge(rope_done, n - 1)
                        m = act.activation(d_xs[:, n % 2, :], PS[:, 2 * j.slot[0] + c, :], ACT.Copy,
                                           scale=0.125 if j.name == "q" else 1.0)
                        if c == 0:
                            m.then_inc(xs_ready, 1)
                    return m
                evacuations(act, "act", jobs, evac)
                phase_end(act, "act")

                def exps(u):
                    act.wait_ge(stat_ready, A.u0 + u + 1)
                    if u >= 3:
                        act.wait_ge(p_ready, u - 2)
                    for c in range(2):
                        n = 2 * (u % 2) + c
                        m = act.activation(d_p[:, u % 3, c, :], PS[:, n, :], ACT.Exp, bias=nmx[:, 2 * (u % 32) + c:2 * (u % 32) + c + 1],
                                           accum_out=rsum[:, 2 * u + c:2 * u + c + 1])
                    m.then_inc(exp_done, 1)
                act_units(act, A, exps)
                phase_end(act, "act")
                load_next(act)
                for t in range(NT):
                    if t >= 3:
                        act.wait_ge(sq_in, t - 2)
                    act.activation(d_p[:, t % 3, :, :].rearrange("p a b -> p (a b)"), d_row[:, t, :], ACT.Square)\
                        .then_inc(sq_done, 1)
                act.wait_ge(sq_in, NT)
                act.activation(rec[:, 0:32], rec[:, 32:64], ACT.Sqrt, scale=1.0 / 128, bias=eps_col[:, 0:1]).then_inc(sd_done, 1)
                phase_end(act, "act")
                act_rows(act, 0, KD)

            def dve(dve, step):
                lv = pcol("lam").rearrange("p (a b d) -> p a b d", a=2, b=2)
                step(dve.tensor_tensor(lam_tmp, lv[:, :, 0, :], lv[:, :, 1, :], ALU.mult))
                dve.tensor_reduce(scol[:, 16:18], lam_tmp, AX_X, ALU.add).then_inc(lam_in, 1)
                dve.wait_ge(lam_exp, 1)
                step(dve.tensor_tensor(scol[:, 20:21], scol[:, 18:19], scol[:, 19:20], ALU.subtract))
                step(dve.tensor_scalar(scol[:, 21:22], scol[:, 20:21], LAM_INIT, None, ALU.add))
                dve.wait_ge(*loads["rope"])
                for n in range(16):
                    dst = (d_tmp[:, 1, :] if n < 8 else d_kT[:, n - 8, :])
                    dve.wait_ge(*xs_in(n))
                    step(dve.tensor_tensor(dst, d_xs[:, n % 2, :], d_cs[:, 0, :], ALU.mult))
                    dve.wait_ge(swapped, n + 1)
                    step(dve.tensor_tensor(d_tmp[:, 0, :], PS[:, 6 + n % 2, :], d_cs[:, 1, :], ALU.mult))
                    if n < 8:
                        step(dve.tensor_tensor(dst, dst, d_tmp[:, 0, :], ALU.add))
                        dve.tensor_scalar(d_qT[:, 2 * n, :], dst, pcol("half", 0, 1), 8.0, ALU.mult, ALU.mult)
                        m = dve.tensor_scalar(d_qT[:, 2 * n + 1, :], dst, pcol("half", 1, 1), 8.0, ALU.mult, ALU.mult)
                        m.then_inc(rope_done, 1)
                        dve.wait_ge(rope_done, n + 1)
                    else:
                        dve.tensor_tensor(dst, dst, d_tmp[:, 0, :], ALU.add).then_inc(rope_done, 1)
                        dve.wait_ge(rope_done, n + 1)
                phase_end(dve, "dve")

                def combine(u):
                    dve.wait_ge(exp_done, A.u0 + u + 1)
                    r0, r1, lr1 = (scol[:, o:o + 1] for o in range(24 + 4 * (u % 2), 27 + 4 * (u % 2)))
                    step(dve.reciprocal(scol[:, 24 + 4 * (u % 2):26 + 4 * (u % 2)], rsum[:, 2 * u:2 * u + 2]))
                    step(dve.tensor_tensor(lr1, r1, scol[:, 21:22], ALU.mult))
                    if u >= 3:
                        dve.wait_ge(pt_psum, A.u0 + u - 2)
                    p1 = d_p[:, u % 3, 1, :]
                    step(dve.tensor_scalar(p1, p1, lr1, None, ALU.mult))
                    dve.scalar_tensor_tensor(out=d_a[:, u % 3, :], in0=d_p[:, u % 3, 0, :], scalar=r0,
                                             in1=p1, op0=ALU.mult, op1=ALU.subtract).then_inc(p_ready, 1)

                def stat(u):
                    dve.wait_ge(s_ready, A.u0 + u + 1)
                    n = 2 * (u % 32)
                    dve.tensor_reduce(nmx[:, n:n + 2], PS[:, 2 * (u % 2):2 * (u % 2) + 2, :], AX_X, ALU.max, negate=True)\
                        .then_inc(stat_ready, 1)
                    if u >= 1:
                        combine(u - 1)
                    if u == A.n - 1:
                        combine(u)

                def store(g, bank):
                    return dve.tensor_copy(d_row[:, g // 2, 512 * (g % 2):512 * (g % 2) + 512], PS[:, bank, :])
                dve_units(dve, A, stat, store)
                phase_end(dve, "dve")
                for t in range(NT):
                    dve.wait_ge(sq_done, t + 1)
                    dve.tensor_reduce(rec[:, 32 + 8 * t:40 + 8 * t],
                                      d_p[:, t % 3, :, :].rearrange("p a (h d) -> p (a h) d", h=4), AX_X, ALU.add)\
                        .then_inc(sq_in, 1)
                dve.wait_ge(sd_done, 1)
                step(dve.reciprocal(rec[:, 32:64], rec[:, 0:32]))
                for t in range(NT):
                    v = d_row[:, t, :].rearrange("p (h d) -> p h d", h=8)
                    step(dve.tensor_tensor(v, v, rec[:, 32 + 8 * t:40 + 8 * t].unsqueeze(2).to_broadcast([P, 8, 128]), ALU.mult))
                    step(dve.scalar_tensor_tensor(out=v, in0=v, scalar=1.0 - LAM_INIT,
                                                  in1=pcol("subln_g").unsqueeze(1).to_broadcast([P, 8, 128]),
                                                  op0=ALU.mult, op1=ALU.mult))
                phase_end(dve, "dve")
                dve_rows(dve, 0, KD)

            def pe(pe):
                pe.wait_ge(*loads["rope"])
                n = [0]

                def swaps(j):
                    for c in range(2):
                        i = n[0]
                        n[0] += 1
                        pe.wait_ge(*xs_in(i))
                        if i >= 2:
                            pe.wait_ge(rope_done, i - 1)
                        pe.matmul(PS[:, 6 + i % 2, :], d_swap[:, :], d_xs[:, i % 2, :], start=True, stop=True,
                                  skip_group_check=True).then_inc(swapped, 1)
                prev = []

                def after(j):
                    if prev:
                        swaps(prev.pop())
                    if j.name in "qk":
                        prev.append(j)
                pe_split(pe, jobs, 1)
                after(jobs[0])
                after(jobs[1])
                pe_projections(pe, rest(jobs), after)
                phase_end(pe, "pe")

                def scores(u, bank):
                    t, h = u // 8, u % 8
                    for c in range(2):
                        m = pe.matmul(PS[:, bank + c, :], d_qT[:, 2 * h + c, chunk(t)], d_kT[:, h, :],
                                      start=True, stop=True, skip_group_check=True)
                    return m

                def values(u, k):
                    h = u % 8
                    return d_v[:, k, 128 * h:128 * h + 128], 128 * (h % 4), 128
                pe_units(pe, A, scores, values, lambda u: (p_ready, u + 1))
                phase_end(pe, "pe")
                phase_end(pe, "pe")
                pe_rows(pe, d_row, 0, KD)
            return {"act_load": act_load, "act": act, "dve": dve, "pe": pe}

        def small_gates_pe(pe, whi_, wlo_, width, bank, ready):
            for t in range(NT):
                for k in range(KD):
                    m = product(pe, PS[:, bank, width * t:width * t + width],
                                (xT_hi[:, k, 128 * t:128 * t + 128], xT_lo[:, k, 128 * t:128 * t + 128]),
                                (whi_[:, k, :], wlo_[:, k, :]), k == 0, k == KD - 1)
            m.then_inc(ready, 1)

        def stage_hgrn(st, jobs):
            A = Units(8 * NT, lambda u: u // 8 + 1, [0, 1, 2, 3], [4, 5], [6, 7], lambda u: u // 8, stat_ready,
                      lambda u: f_p[:, u % 3, :], lambda u: f_pt[:, u % 2, :], lambda u: u % 8 == 7)
            names = ["f_cut", "f_sum", "f_abs", "f_ln", "f_cols", "f_rows_ps", "f_scan", "f_bc", "f_bc_read",
                     "lb_in", "lb_exp", "lb_done", "g_lf", "g_scan", "g_din", "g_exp", "g_ops", "g_sc", "g_msk", "g_o",
                     "g_kht", "g_khc", "g_kv", "g_st", "g_store", "gq_in", "gq_done", "gs_in", "gs_done"]
            G = {n: S_(n) for n in names}
            chunk = lambda c: slice(128 * c, 128 * c + 128)
            NL = 8

            def act_load(act):
                load(act, "levels", f_w[:, :, :], a["ev_w_in_2"][:, 3584:3592].rearrange("(k p) c -> p k c", p=P))
                load(act, "levels", g_lev[:, :, :], a["levels"])

            def act(act, step):
                act.wait_ge(G["f_abs"], 1)
                step(act.activation(f_tmp[:, 0, :, :], f_tmp[:, 0, :, :], ACT.Exp, scale=-1.0))
                act.activation(f_tmp[:, 0, :, :], f_tmp[:, 0, :, :], ACT.Ln, bias=one_col[:, 0:1]).then_inc(G["f_ln"], 1)
                act.wait_ge(G["lb_in"], 1)
                act.activation(scol[:, 0:12], scol[:, 0:12], ACT.Exp).then_inc(G["lb_exp"], 1)

                def evac(j):
                    s = j.slot[0]
                    for c in range(2 if j.name in ("q", "z", "fq") else 0):
                        i = j.i + c
                        src = PS[:, 2 * s + c, :]
                        if j.name == "q":
                            m = act.activation(g_qT[:, i, :], src, ACT.Copy)
                        elif j.name == "z":
                            act.activation(g_b[:, i, :], src, ACT.Sigmoid)
                            m = act.activation(g_kT[:, i, :], src, ACT.Sigmoid, scale=-1.0)
                        else:
                            for hh in range(2):
                                m = act.activation(f_qT[:, 2 * i + hh, :], src, ACT.Copy, scale=pcol("half", hh, 1))
                    if j.name == "g":
                        for t in range(NT):
                            m = act.activation(g_g[:, t, :], PS[:, 2 * j.slot[t // 2] + t % 2, :], ACT.Silu)
                    return m
                evacuations(act, "act", jobs, evac)
                phase_end(act, "act")
                for i in range(4):
                    act.activation(g_b[:, i, :], g_b[:, i, :], ACT.Ln, scale=scol[:, 36 + i:37 + i],
                                   bias=scol[:, 32 + i:33 + i]).then_inc(G["g_lf"], 1)
                ne = 0
                for h in range(4):
                    for l in range(1, NL + 2):
                        act.wait_ge(G["g_din"], ne + 1)
                        if ne >= 2:
                            act.wait_ge(G["g_ops"], ne - 1)
                        e = g_e[:, ne % 2, :]
                        if l < NL:
                            step(act.activation(e, g_d2[:, ne % 2, :], ACT.Abs))
                            act.activation(e, e, ACT.Exp, scale=-1.0).then_inc(G["g_exp"], 1)
                        else:
                            act.activation(e, g_d2[:, ne % 2, :] if l > NL else g_b[:, h, :], ACT.Exp).then_inc(G["g_exp"], 1)
                        ne += 1
                    act.wait_ge(G["g_kht"], h + 1)
                    if h >= 1:
                        act.wait_ge(G["g_kv"], h)
                    act.activation(g_khr[:, :], PS[:, 4, :], ACT.Copy).then_inc(G["g_khc"], 1)
                phase_end(act, "act")
                for t in range(NT):
                    act.activation(g_e4[:, t, :], g_row[:, t, 0:512], ACT.Square).then_inc(G["gq_done"], 1)
                act.wait_ge(G["gs_in"], 1)
                act.activation(scol[:, 16:32], scol[:, 0:16], ACT.Sqrt, scale=1.0 / 128, bias=eps_col[:, 0:1])\
                    .then_inc(G["gs_done"], 1)
                phase_end(act, "act")
                for h in range(8):
                    act.wait_ge(G["f_bc"], h + 1)
                    act.activation(f_c[:, h, :], PS[:, 4 + h % 4, :], ACT.Copy).then_inc(G["f_bc_read"], 1)
                phase_end(act, "act")
                act_units(act, A, lambda u: softmax_exp(act, A, u, f_add[:, u % 2, 0:128 * A.nk(u)], -1.0,
                                                        128 * A.nk(u), A.p(u)))
                phase_end(act, "act")
                act_rows(act, 0, KD)

            def dve(dve, step):
                dve.wait_ge(*loads["levels"])
                step(dve.tensor_copy(f_whi[:, :, :], f_w[:, :, :]))
                dve.tensor_tensor(f_wlo[:, :, :], f_w[:, :, :], f_whi[:, :, :].bitcast(F32), ALU.subtract)\
                    .then_inc(G["f_cut"], 1)
                dve.wait_ge(G["f_sum"], 1)
                step(dve.tensor_tensor(f_col[:, :, :], PS[:, 7, 0:32].rearrange("p (t g) -> p t g", t=NT),
                                       pcol("fox_b").unsqueeze(1).to_broadcast([P, NT, 8]), ALU.add))
                dve.tensor_scalar(f_tmp[:, 1, :, :], f_col[:, :, :], 0.0, None, ALU.min)
                dve.scalar_tensor_tensor(out=f_tmp[:, 0, :, :], in0=f_col[:, :, :], scalar=-1.0, in1=f_col[:, :, :],
                                         op0=ALU.mult, op1=ALU.max).then_inc(G["f_abs"], 1)
                dve.wait_ge(G["f_ln"], 1)
                dve.tensor_tensor(f_col[:, :, :], f_tmp[:, 1, :, :], f_tmp[:, 0, :, :], ALU.subtract)\
                    .then_inc(G["f_cols"], 1)
                lb = pcol("hgrn_lb").rearrange("p (r k) -> p r k", r=3)
                e3 = scol[:, 0:12].rearrange("p (r k) -> p r k", r=3)
                step(dve.tensor_tensor(scol[:, 12:16], lb[:, 0, :], lb[:, 1, :], ALU.max))
                step(dve.tensor_tensor(scol[:, 12:16], scol[:, 12:16], lb[:, 2, :], ALU.max))
                dve.tensor_tensor(e3, lb, scol[:, 12:16].unsqueeze(1).to_broadcast([P, 3, 4]), ALU.subtract)\
                    .then_inc(G["lb_in"], 1)
                dve.wait_ge(G["lb_exp"], 1)
                step(dve.tensor_tensor(scol[:, 16:20], e3[:, 0, :], e3[:, 1, :], ALU.add))
                step(dve.tensor_tensor(scol[:, 16:20], scol[:, 16:20], e3[:, 2, :], ALU.add))
                step(dve.reciprocal(scol[:, 20:24], scol[:, 16:20]))
                step(dve.tensor_tensor(scol[:, 32:36], e3[:, 0, :], scol[:, 20:24], ALU.mult))
                step(dve.tensor_scalar(scol[:, 36:40], scol[:, 32:36], -1.0, 1.0, ALU.mult, ALU.add))

                def evac(j):
                    if j.name == "fk":
                        for c in range(2):
                            m = dve.tensor_copy(f_kT[:, j.i + c, :], PS[:, 2 * j.slot[0] + c, :])
                        return m
                    dst = g_v if j.name == "v" else f_v
                    for t in range(NT):
                        m = dve.tensor_copy(dst[:, t, :], PS[:, 2 * j.slot[t // 2] + t % 2, :])
                    return m
                evacuations(dve, "dve", jobs, evac)
                phase_end(dve, "dve")
                step(dve.memset(g_rst[:, :], 1.0))
                step(dve.memset(g_rst[:, 0:S:128], 0.0))
                for i in range(4):
                    dve.tensor_scalar(g_kT[:, i, :], g_kT[:, i, :], scol[:, 36 + i:37 + i], None, ALU.mult)
                    dve.wait_ge(G["g_lf"], i + 1)
                    step(dve.tensor_tensor_scan(g_b[:, i, :], g_rst[:, :], g_b[:, i, :], 0.0, ALU.mult, ALU.add))

                EX = [(h, l) for h in range(4) for l in range(1, NL + 2)]

                def diff(i):
                    h, l = EX[i]
                    if i >= 2:
                        dve.wait_ge(G["g_exp"], i - 1)
                    b = g_b[:, h, :]
                    if l < NL:
                        m_ = 1 << (l - 1)
                        v = b.rearrange("p (g w) -> p g w", w=2 * m_)
                        ref = v[:, :, m_ - 1:m_].to_broadcast([P, S // (2 * m_), 2 * m_])
                        m = dve.tensor_tensor(g_d2[:, i % 2, :].rearrange("p (g w) -> p g w", w=2 * m_), v, ref, ALU.subtract)
                    elif l == NL:
                        m = dve.memset(scol[:, 63:64], 0.0)
                    else:
                        v = b.rearrange("p (g w) -> p g w", w=128)
                        m = dve.tensor_tensor(g_d2[:, i % 2, :].rearrange("p (g w) -> p g w", w=128),
                                              v[:, :, 127:128].to_broadcast([P, NT, 128]), v, ALU.subtract)
                    m.then_inc(G["g_din"], 1)

                def mask(n):
                    dve.wait_ge(G["g_sc"], n + 1)
                    if n >= 2:
                        dve.wait_ge(G["g_o"], n - 1)
                    dve.tensor_tensor(g_s[:, n % 2, :].rearrange("p (c l) -> p c l", c=NT),
                                      PS[:, n % 2, :].rearrange("p (c l) -> p c l", c=NT),
                                      g_lev[:, n % NL, :].unsqueeze(1).to_broadcast([P, NT, P]), ALU.mult)\
                        .then_inc(G["g_msk"], 1)
                diff(0)
                diff(1)
                for i, (h, l) in enumerate(EX):
                    e = g_e[:, i % 2, :]
                    dve.wait_ge(G["g_exp"], i + 1)
                    if l < NL:
                        n = h * NL + l
                        if n >= 2:
                            dve.wait_ge(G["g_sc"], n - 1)
                        dve.tensor_tensor(g_qe[:, n % 2, :], g_qT[:, h, :], e, ALU.mult)
                        dve.tensor_tensor(g_ke[:, n % 2, :], g_kT[:, h, :], e, ALU.mult).then_inc(G["g_ops"], 1)
                        mask(n - 1)
                        if l == NL - 1:
                            mask(n)
                    elif l == NL:
                        dve.tensor_copy(scol[:, 40 + 4 * (h % 2):44 + 4 * (h % 2)], e[:, 127:S:128])
                        dve.tensor_tensor(g_qh[:, :], g_qT[:, h, :], e, ALU.mult).then_inc(G["g_ops"], 1)
                    else:
                        dve.tensor_tensor(g_kh[:, :], g_kT[:, h, :], e, ALU.mult).then_inc(G["g_ops"], 1)
                    if i + 2 < len(EX):
                        diff(i + 2)
                    if l == NL + 1:
                        dve.wait_ge(G["g_kv"], h + 1)
                        step(dve.tensor_copy(g_state[:, 1, :], PS[:, 5, 0:128]))
                        dc = 40 + 4 * (h % 2)
                        step(dve.scalar_tensor_tensor(out=g_state[:, 2, :], in0=g_state[:, 1, :], scalar=scol[:, dc + 1:dc + 2],
                                                      in1=PS[:, 5, 128:256], op0=ALU.mult, op1=ALU.add))
                        dve.scalar_tensor_tensor(out=g_state[:, 3, :], in0=g_state[:, 2, :], scalar=scol[:, dc + 2:dc + 3],
                                                 in1=PS[:, 5, 256:384], op0=ALU.mult, op1=ALU.add).then_inc(G["g_st"], 1)
                        dve.wait_ge(G["gq_in"], h + 1)
                        dve.tensor_copy(g_row[:, :, 128 * h:128 * h + 128],
                                        PS[:, 2 + h % 2, :].rearrange("p (t e) -> p t e", t=NT)).then_inc(G["g_store"], 1)
                phase_end(dve, "dve")
                for t in range(NT):
                    dve.wait_ge(G["gq_done"], t + 1)
                    m = dve.tensor_reduce(scol[:, 4 * t:4 * t + 4], g_e4[:, t, :].rearrange("p (h d) -> p h d", h=4),
                                          AX_X, ALU.add)
                m.then_inc(G["gs_in"], 1)
                dve.wait_ge(G["gs_done"], 1)
                step(dve.reciprocal(scol[:, 0:16], scol[:, 16:32]))
                for t in range(NT):
                    v = g_row[:, t, 0:512].rearrange("p (h d) -> p h d", h=4)
                    step(dve.tensor_tensor(v, v, scol[:, 4 * t:4 * t + 4].unsqueeze(2).to_broadcast([P, 4, 128]), ALU.mult))
                    step(dve.tensor_tensor(v, v, pcol("norm_g").unsqueeze(1).to_broadcast([P, 4, 128]), ALU.mult))
                    dve.tensor_tensor(g_row[:, t, 0:512], g_row[:, t, 0:512], g_g[:, t, :], ALU.mult)
                phase_end(dve, "dve")
                step(dve.memset(f_rows[:, :], 0.0))
                step(dve.memset(f_zero[:, :], 0.0))
                dve.wait_ge(G["f_rows_ps"], 1)
                dve.tensor_tensor_scan(f_rows[0:8, :], f_zero[0:8, :], PS[0:8, 0, :], 0.0, ALU.add, ALU.subtract)\
                    .then_inc(G["f_scan"], 1)
                phase_end(dve, "dve")

                def stat(u):
                    t, h = u // 8, u % 8
                    n = 128 * (t + 1)
                    dve.wait_ge(s_ready, A.u0 + u + 1)
                    if u >= 2:
                        dve.wait_ge(exp_done, A.u0 + u - 1)
                    dve.tensor_tensor_reduce(out=f_add[:, u % 2, 0:n], in0=PS[:, A.ps(u), 0:n], in1=f_c[:, h, 0:n],
                                             scale=-1.0, scalar=-NEG, op0=ALU.add, op1=ALU.min,
                                             accum_out=nmx[:, u:u + 1]).then_inc(stat_ready, 1)

                def store(g, bank):
                    step(dve.reciprocal(rec[:, 8 * g:8 * g + 8], rsum[:, 8 * g:8 * g + 8]))
                    return dve.tensor_tensor(g_row[:, g, 512:1024].rearrange("p (h d) -> p h d", h=8),
                                             PS[:, bank, :].rearrange("p (h d) -> p h d", h=8),
                                             rec[:, 8 * g:8 * g + 8].unsqueeze(2).to_broadcast([P, 8, 64]), ALU.mult)
                dve_units(dve, A, stat, store)
                phase_end(dve, "dve")
                dve_rows(dve, 0, KD)

            def pe(pe):
                pe_split(pe, jobs, 1)
                pe.wait_ge(G["f_cut"], 1)
                small_gates_pe(pe, f_whi, f_wlo, 8, 7, G["f_sum"])
                pe_projections(pe, jobs[2:3])
                pe.wait_ge(G["f_cols"], 1)
                pe_projections(pe, jobs[3:])
                phase_end(pe, "pe")
                for h in range(4):
                    ob = 2 + h % 2
                    if h >= 2:
                        pe.wait_ge(G["g_store"], h - 1)

                    def outs(n, first):
                        pe.wait_ge(G["g_msk"], n + 1)
                        for c in range(NT):
                            m = pe.matmul(PS[:, ob, chunk(c)], g_s[:, n % 2, chunk(c)], g_v[:, c, 128 * h:128 * h + 128],
                                          start=first and c == 0, stop=False, skip_group_check=True)
                        m.then_inc(G["g_o"], 1)
                    for l in range(NL):
                        n = h * NL + l
                        if n >= 2:
                            pe.wait_ge(G["g_msk"], n - 1)
                        if l == 0:
                            if h == 0:
                                pe.wait_ge(G["g_ops"], 1)
                            q_, k_ = g_qT[:, h, :], g_kT[:, h, :]
                        else:
                            pe.wait_ge(G["g_ops"], h * (NL + 1) + l)
                            q_, k_ = g_qe[:, n % 2, :], g_ke[:, n % 2, :]
                        for c in range(NT):
                            m = pe.matmul(PS[:, n % 2, chunk(c)], k_[:, chunk(c)], q_[:, chunk(c)], start=True, stop=True,
                                          skip_group_check=True)
                        m.then_inc(G["g_sc"], 1)
                        if l >= 1:
                            outs(n - 1, l == 1)
                    outs(h * NL + NL - 1, False)
                    pe.wait_ge(G["g_ops"], (h + 1) * (NL + 1))
                    for c in range(NT):
                        m = pe.transpose(PS[:, 4, chunk(c)], g_kh[:, chunk(c)], ident)
                    m.then_inc(G["g_kht"], 1)
                    pe.wait_ge(G["g_khc"], h + 1)
                    for c in range(3):
                        m = pe.matmul(PS[:, 5, chunk(c)], g_khr[:, chunk(c)], g_v[:, c, 128 * h:128 * h + 128],
                                      start=True, stop=True, skip_group_check=True)
                    m.then_inc(G["g_kv"], 1)
                    pe.wait_ge(G["g_st"], h + 1)
                    for c in range(1, NT):
                        m = pe.matmul(PS[:, ob, chunk(c)], g_qh[:, chunk(c)], g_state[:, c, :], start=False, stop=c == NT - 1,
                                      skip_group_check=True)
                    m.then_inc(G["gq_in"], 1)
                phase_end(pe, "pe")
                phase_end(pe, "pe")
                for t in range(NT):
                    m = pe.transpose(PS[0:8, 0, chunk(t)], f_col[:, t, :], ident)
                m.then_inc(G["f_rows_ps"], 1)
                pe.wait_ge(G["f_scan"], 1)
                for h in range(8):
                    if h >= 4:
                        pe.wait_ge(G["f_bc_read"], h - 3)
                    pe.matmul(PS[:, 4 + h % 4, :], ident[:, h:h + 1].to_broadcast([P, P]), f_rows[:, :], start=True, stop=True,
                              skip_group_check=True).then_inc(G["f_bc"], 1)
                phase_end(pe, "pe")

                def scores(u, bank):
                    t, h = u // 8, u % 8
                    pe.matmul(PS[:, bank, 0:128 * (t + 1)], f_qT[:, h, chunk(t)], f_kT[:, h // 2, 0:128 * (t + 1)],
                              start=True, stop=False, skip_group_check=True)
                    return pe.matmul(PS[:, bank, chunk(t)], ident, pcol("le"), start=False, stop=True,
                                     skip_group_check=True)

                def values(u, k):
                    h = u % 8
                    return f_v[:, k, 64 * h:64 * h + 64], 64 * h, 64
                pe_units(pe, A, scores, values, lambda u: (exp_done, A.u0 + u + 1))
                phase_end(pe, "pe")
                pe_rows(pe, g_row, 0, KD)
            return {"act_load": act_load, "act": act, "dve": dve, "pe": pe}

        def stage_lru(st, jobs):
            A = Units(8 * NT, lambda u: u // 8 + 1, [0, 1, 2, 3], [4, 5], [6, 7], lambda u: u // 8, exp_done,
                      lambda u: s_p[:, u % 3, :], lambda u: s_pt[:, u % 2, :], lambda u: u % 8 == 7)
            names = ["l_pre_in", "l_conv", "l_gates", "l_act1", "l_act2", "l_om", "l_sq", "l_h", "l_hi", "sp_in", "sp_ln",
                     "l_c"]
            G = {n: S_(n) for n in names}
            chunk = lambda c: slice(128 * c, 128 * c + 128)

            def act_load(act):
                load(act, "lru_w", l_w[:, :, :, :], a["lru_gates"])

            def act(act, step):
                act.wait_ge(G["sp_in"], 1)
                step(act.activation(scol[:, 0:4], scol[:, 0:4], ACT.Exp, scale=-1.0))
                act.activation(scol[:, 0:4], scol[:, 0:4], ACT.Ln, bias=one_col[:, 0:1]).then_inc(G["sp_ln"], 1)

                def evac(j):
                    s = j.slot[0]
                    for c in range(2):
                        i = j.i + c
                        src = PS[:, 2 * s + c, :]
                        if j.name == "x":
                            m = act.activation(l_pre[:, i, 3:3 + S], src, ACT.Copy)
                        elif j.name == "g":
                            m = act.activation(l_g[:, i, :], src, ACT.Gelu_apprx_tanh)
                        else:
                            for hh in range(2):
                                m = act.activation(s_qT[:, 2 * i + hh, :], src, ACT.Copy, scale=pcol("half", hh, 1))
                    return m
                evacuations(act, "act", jobs, evac)
                phase_end(act, "act")
                for i in range(4):
                    act.wait_ge(G["l_gates"], i + 1)
                    act.activation(l_r[:, i, :], PS[:, 2 * (i % 4), :], ACT.Sigmoid, bias=pcol("lru_ba", i, 1))
                    act.activation(l_i[:, i, :], PS[:, 2 * (i % 4) + 1, :], ACT.Sigmoid, bias=pcol("lru_bx", i, 1))\
                        .then_inc(G["l_act1"], 1)
                act.wait_ge(G["l_act1"], 4)
                act.wait_ge(G["l_c"], 1)
                for i in range(4):
                    act.activation(l_a[:, i, :], l_r[:, i, :], ACT.Exp, scale=scol[:, 8 + i:9 + i])
                    act.activation(l_t[:, i, :], l_r[:, i, :], ACT.Tanh, scale=scol[:, 12 + i:13 + i]).then_inc(G["l_act2"], 1)
                for i in range(4):
                    act.wait_ge(G["l_om"], i + 1)
                    act.activation(l_t[:, i, :], l_t[:, i, :], ACT.Sqrt).then_inc(G["l_sq"], 1)
                for i in range(4):
                    act.wait_ge(G["l_h"], i + 1)
                    act.activation(xT_hi[:, i, :], l_r[:, i, :], ACT.Copy).then_inc(G["l_hi"], 1)
                phase_end(act, "act")

                def exps(u):
                    n = 128 * A.nk(u)
                    act.wait_ge(s_ready, A.u0 + u + 1)
                    if u >= 2:
                        act.wait_ge(stat_ready, A.u0 + u - 1)
                    act.activation(s_pos[:, u % 2, 0:n], PS[:, A.ps(u), 0:n], ACT.Sigmoid)
                    act.activation(s_neg[:, u % 2, 0:n], PS[:, A.ps(u), 0:n], ACT.Sigmoid, scale=-1.0)\
                        .then_inc(exp_done, 1)
                act_units(act, A, exps)
                phase_end(act, "act")
                act_rows(act, 4, 4)

            def dve(dve, step):
                dve.memset(l_pre[:, :, 0:3], 0.0)
                dve.tensor_scalar(scol[:, 4:8], pcol("lru_lam"), -1.0, 0.0, ALU.mult, ALU.max)
                dve.scalar_tensor_tensor(out=scol[:, 0:4], in0=pcol("lru_lam"), scalar=-1.0, in1=pcol("lru_lam"), op0=ALU.mult,
                                         op1=ALU.max).then_inc(G["sp_in"], 1)
                dve.wait_ge(G["sp_ln"], 1)
                step(dve.tensor_tensor(scol[:, 0:4], scol[:, 0:4], scol[:, 4:8], ALU.add))
                dve.tensor_scalar(scol[:, 8:12], scol[:, 0:4], -8.0, None, ALU.mult)
                dve.tensor_scalar(scol[:, 12:16], scol[:, 0:4], 8.0, None, ALU.mult).then_inc(G["l_c"], 1)

                def evac(j):
                    if j.name == "k":
                        for c in range(2):
                            m = dve.tensor_copy(s_kT[:, j.i + c, :], PS[:, 2 * j.slot[0] + c, :])
                        return m
                    for t in range(NT):
                        m = dve.tensor_copy(s_v[:, t, :], PS[:, 2 * j.slot[t // 2] + t % 2, :])
                    return m
                evacuations(dve, "dve", jobs, evac)
                phase_end(dve, "dve")
                for i in range(4):
                    o, src = l_xc[:, i, :], l_pre[:, i, :]
                    step(dve.tensor_scalar(o, src[:, 0:S], pcol("lru_w", i, 1), pcol("lru_b", i, 1), ALU.mult, ALU.add))
                    for k in range(1, 4):
                        m = dve.scalar_tensor_tensor(out=o, in0=src[:, k:k + S], scalar=pcol("lru_w", 4 * k + i, 1), in1=o,
                                                     op0=ALU.mult, op1=ALU.add)
                        if k < 3:
                            step(m)
                    m.then_inc(G["l_conv"], 1)
                for i in range(4):
                    dve.wait_ge(G["l_act1"], i + 1)
                    step(dve.tensor_tensor(l_i[:, i, :], l_i[:, i, :], l_xc[:, i, :], ALU.mult))
                for i in range(4):
                    dve.wait_ge(G["l_act2"], i + 1)
                    r, t_ = l_r[:, i, :], l_t[:, i, :]
                    step(dve.tensor_scalar(r, t_, 1.0, None, ALU.add))
                    step(dve.reciprocal(r, r))
                    dve.scalar_tensor_tensor(out=t_, in0=t_, scalar=2.0, in1=r, op0=ALU.mult, op1=ALU.mult)\
                        .then_inc(G["l_om"], 1)
                for i in range(4):
                    dve.wait_ge(G["l_sq"], i + 1)
                    x_, r = l_i[:, i, :], l_r[:, i, :]
                    step(dve.tensor_tensor(x_, x_, l_t[:, i, :], ALU.mult))
                    step(dve.tensor_tensor_scan(r, l_a[:, i, :], x_, 0.0, ALU.mult, ALU.add))
                    dve.tensor_tensor(r, r, l_g[:, i, :], ALU.mult).then_inc(G["l_h"], 1)
                    dve.wait_ge(G["l_h"], i + 1)
                for i in range(4):
                    dve.wait_ge(G["l_hi"], i + 1)
                    dve.tensor_tensor(xT_lo[:, i, :], l_r[:, i, :], xT_hi[:, i, :].bitcast(F32), ALU.subtract)
                phase_end(dve, "dve")
                dve.memset(s_mask[:, 0:S - 128], 0.0)
                dve.memset(s_c[:, :, S:S + 1], 1.0)
                step(dve.tensor_scalar(s_mask[:, S - 128:S], pcol("strict"), -1.0, 1.0, ALU.mult, ALU.add))

                def stat(u):
                    n = 128 * A.nk(u)
                    c, p_ = s_c[:, u % 2, :], s_p[:, u % 3, 0:n]
                    dve.wait_ge(exp_done, A.u0 + u + 1)
                    step(dve.tensor_tensor_scan(c[:, S - n:S][:, ::-1], s_neg[:, u % 2, 0:n][:, ::-1],
                                                s_mask[:, S - n:S][:, ::-1], 1.0, ALU.mult, ALU.max))
                    if u >= 3:
                        dve.wait_ge(pt_psum, A.u0 + u - 2)
                    step(dve.tensor_tensor(p_, s_pos[:, u % 2, 0:n], c[:, S - n + 1:S + 1], ALU.mult))
                    dve.tensor_tensor(p_[:, n - 128:n], p_[:, n - 128:n], pcol("strict"), ALU.mult)\
                        .then_inc(stat_ready, 1)

                def store(g, bank):
                    return dve.tensor_copy(s_row[:, g, :], PS[:, bank, :])
                dve_units(dve, A, stat, store)
                phase_end(dve, "dve")
                dve_rows(dve, 4, 4)

            def pe(pe):
                pe_split(pe, jobs, 1)
                pe_projections(pe, rest(jobs))
                phase_end(pe, "pe")
                pe.wait_ge(*loads["lru_w"])
                for i in range(4):
                    pe.wait_ge(G["l_conv"], i + 1)
                    for g in range(2):
                        m = pe.matmul(PS[:, 2 * i + g, :], l_w[:, g, i, :], l_xc[:, i, :], start=True, stop=True,
                                      skip_group_check=True)
                    m.then_inc(G["l_gates"], 1)
                phase_end(pe, "pe")

                def scores(u, bank):
                    t, h = u // 8, u % 8
                    return pe.matmul(PS[:, bank, 0:128 * (t + 1)], s_qT[:, h, chunk(t)], s_kT[:, h // 2, 0:128 * (t + 1)],
                                     start=True, stop=True, skip_group_check=True)

                def values(u, k):
                    h = u % 8
                    return s_v[:, k, 64 * h:64 * h + 64], 64 * h, 64
                pe_units(pe, A, scores, values, lambda u: (stat_ready, A.u0 + u + 1))
                phase_end(pe, "pe")
                pe_rows(pe, s_row, 4, 4)
            return {"act_load": act_load, "act": act, "dve": dve, "pe": pe}

        makers = {"even": stage_even, "cross": stage_cross, "ffn": stage_ffn, "odd": stage_odd, "hgrn": stage_hgrn,
                  "lru": stage_lru}
        code = []
        for n, (st, jobs) in enumerate(program):
            c = makers[st[0]](st, jobs)
            c["kind"] = st[0]
            c["ln"] = st[-1]
            c.setdefault("head", {"pe": lambda pe, turns, jobs=jobs: pe_split(pe, jobs, 0, turns),
                                  "act": lambda act, turns: turns(), "dve": lambda dve, turns: turns()})
            c.setdefault("lhs", (xT_hi, xT_lo, KD))
            code.append(c)

        block = ctx.enter_context(nc.Block())

        @block.sync
        def _(sp):
            for n, src in enumerate(panels):
                if n >= 2:
                    sp.wait_ge(panel_split, n - 1)
                nk = src.shape[1]
                sp.dma_start(raw[n % 2][:, :].rearrange("p (k c) -> p k c", k=nk), src).then_inc(panel_loaded[n % 2], 16)

        @block.gpsimd
        def _(pool):
            for n in range(len(panels)):
                b = n % 2
                pool.wait_ge(panel_loaded[b], 16 * (n // 2 + 1))
                if n >= 2:
                    pool.wait_ge(*panel_done[n - 2])
                pool.tensor_scalar(whi[b][:, :], raw[b][:, :], 1.0, 1.0, ALU.mult, ALU.mult).then_inc(panel_hi, 1)
                pool.wait_ge(panel_hi, n + 1)
                pool.tensor_tensor(wlo[b][:, :], raw[b][:, :], whi[b][:, :].bitcast(F32), ALU.subtract)\
                    .then_inc(panel_split, 1)

        @block.scalar
        def _(act):
            step = stepper(act, act_step)
            act.dma_start(par[:, :], a["par"]).then_inc(inputs_in, 16)
            act.dma_start(x_row[:, :, :], a["x"].rearrange("(t p) d -> p t d", p=P)).then_inc(inputs_in, 16)
            code[0]["act_load"](act)
            for t in (0, 1):
                act_turn(act, xT_hi, 0, KD, 2 * t, t)
            code[0]["head"]["act"](act, lambda: [act_turn(act, xT_hi, 0, KD, 2 * t, t) for t in (2, 3)])
            for i, c in enumerate(code):
                at_stage[0] = i
                load(act, f"ln{i}", ln_gb[:, 0, :], c["ln"][0].partition_broadcast(P))
                load(act, f"ln{i}", ln_gb[:, 1, :], c["ln"][1].partition_broadcast(P))
                c["act"](act, step)
                nxt = code[i + 1] if i + 1 < len(code) else None
                if nxt and "memory" in nxt:
                    nxt["memory"]["act"](act)
                act_block_out(act, nxt and nxt["head"]["act"])
                if c["kind"] == "ffn":
                    load_next(act)

        @block.vector
        def _(dve):
            step = stepper(dve, dve_step)
            dve.memset(eps_col[:, :], EPS)
            dve.memset(one_col[:, :], 1.0)
            dve.wait_ge(inputs_in, 32)
            for t in (0, 1):
                dve_turn(dve, xT_hi, xT_lo, 0, KD, 2 * t, t)
            code[0]["head"]["dve"](dve, lambda: [dve_turn(dve, xT_hi, xT_lo, 0, KD, 2 * t, t) for t in (2, 3)])
            for i, c in enumerate(code):
                c["dve"](dve, step)
                nxt = code[i + 1] if i + 1 < len(code) else None
                if nxt and "memory" in nxt:
                    nxt["memory"]["dve"](dve)
                dve_block_out(dve, step, nxt and nxt["head"]["dve"], loads[f"ln{i}"])

        @block.tensor
        def _(pe):
            pe.wait_ge(inputs_in, 32)
            for t in (0, 1):
                pe_turn(pe, x_row[:, t, :], KD, 2 * t)
            code[0]["head"]["pe"](pe, lambda: [pe_turn(pe, x_row[:, t, :], KD, 2 * t) for t in (2, 3)])
            for i, c in enumerate(code):
                c["pe"](pe)
                nxt = code[i + 1] if i + 1 < len(code) else None
                if "free" in c:
                    first = [(k, evac_dve, v) for v, k in c["free"]]
                else:
                    first = [(t, lo_ready, n_turn["pe"] - NT + t + 1) for t in range(NT)]
                if nxt and "memory" in nxt:
                    nxt["memory"]["pe"](pe)
                    first = first[MT:] + [(t, lo_ready, n_turn["pe"] - MT + t + 1) for t in range(MT)]
                pe_block_out(pe, first, *c["lhs"], nxt and nxt["head"]["pe"])
            assert used[0] == len(panels) == len(panel_done), (used[0], len(panels), len(panel_done))


def host_par(i):
    n = np.arange(P)
    f = np.float32

    def tiles(v, k):
        return v.reshape(-1, k, P).transpose(2, 0, 1).reshape(P, -1)

    def copies(v):
        return np.broadcast_to(v.reshape(1, -1), (P, v.size))

    col, part = n[None, :], n[:, None]
    blocks = {
        "ident": np.eye(P, dtype=f),
        "ge": np.where(col >= part, f(0), f(NEG)),
        "le": np.where(col <= part, f(0), f(NEG)),
        "strict": np.where(col < part, f(1), f(0)),
        "gate_b": copies(i["even_gate_b"]),
        "conv_w": tiles(i["even_conv_w"][0], 8),
        "subln_g": copies(i["odd_subln_g"]),
        "lam": copies(i["odd_lambda"]),
        "fox_b": copies(i["ev_fox_bf_2"]),
        "hgrn_lb": tiles(i["hgrn_lb_2"], 4),
        "norm_g": copies(i["ev_hgrn_norm_g_2"]),
        "lru_w": tiles(i["od_conv_w_2"][0], 4),
        "lru_b": tiles(i["od_conv_b_2"], 4),
        "lru_ba": tiles(i["od_gate_a_b_2"], 4),
        "lru_bx": tiles(i["od_gate_x_b_2"], 4),
        "lru_lam": tiles(i["od_lru_lambda_2"], 4),
        "half": np.stack([np.where(n < 64, f(0.125), f(0)), np.where(n >= 64, f(0.125), f(0))], 1),
    }
    assert {k: v.shape[1] for k, v in blocks.items()} == {k: v[1] for k, v in PAR.items()}
    return np.ascontiguousarray(np.concatenate([blocks[k] for k in PAR], 1).astype(f))


def host_constants():
    f = np.float32
    n = np.arange(P)
    freq = 10000.0 ** (-np.arange(0, 64, 2, dtype=f) / f(64))
    ang = freq.astype(f)[n % 32][:, None] * np.arange(S, dtype=f)[None, :]
    sign = np.where(n % 64 < 32, f(-1), f(1))[:, None]
    rope = np.stack([np.cos(ang), sign * np.sin(ang)], 1).astype(f)
    swap = np.zeros((P, P), f)
    swap[n, n ^ 32] = 1
    c = n % 64
    start = np.clip(c - 8, 0, 48)
    k = np.arange(64)
    inside = (k[None, :] >= start[:, None]) & (k[None, :] < start[:, None] + 16)
    winmask = np.where(inside, f(0), f(NEG))
    s_, t_ = n[:, None], n[None, :]
    levels = [s_ == t_]
    for l in range(1, 8):
        m = 1 << (l - 1)
        levels.append((s_ // (2 * m) == t_ // (2 * m)) & (s_ % (2 * m) < m) & (t_ % (2 * m) >= m))
    levels = np.stack(levels, 1).astype(f)
    return {"rope": rope, "swap": swap, "winmask": winmask, "levels": np.ascontiguousarray(levels)}


def host_arrays(i):
    f = np.float32
    big = ["even_w_in", "even_w_out", "odd_w_in", "odd_w_out", "ev_w_in_2", "ev_w_out_2", "od_w_in_2", "od_w_out_2"]
    arrays = {k: np.ascontiguousarray(i[k][0]) for k in big}
    for k in ("mem_wq", "mem_wkv", "mem_wo", "ffn_w_gu", "ffn_w_down", "ffn_w13_2", "ffn_w2_2", "ln_g", "ln_b",
              "ln_g_2", "ln_b_2"):
        arrays[k] = np.ascontiguousarray(i[k])
    arrays["x"] = np.ascontiguousarray(i["x"][0])
    arrays["mem"] = np.ascontiguousarray(i["mem"][0])
    arrays["par"] = host_par(i)
    arrays.update(host_constants())
    pad = np.zeros((8, 17, 127), f)
    pad[:, 1:16, 48:79] = i["even_rpb"][0]
    half, c = np.arange(P)[:, None, None] // 64, np.arange(P)[:, None, None] % 64
    arrays["rpb"] = np.ascontiguousarray(pad[:, 1 - half + np.arange(16)[None, :, None],
                                             63 - c + np.arange(64)[None, None, :]])
    gates = np.zeros((P, 2, 4, P), f)
    for g, k in enumerate(("od_gate_a_w_2", "od_gate_x_w_2")):
        for b in range(8):
            o = 64 * (b % 2)
            gates[o:o + 64, g, b // 2, o:o + 64] = i[k][0, b]
    arrays["lru_gates"] = gates
    return arrays


def all_stages(a):
    def ln(name, l, k):
        g, b = (a["ln_g"], a["ln_b"]) if name == 1 else (a["ln_g_2"], a["ln_b_2"])
        return g[l, k, :], b[l, k, :]
    return [
        ("even", ln(1, 0, 0)), ("cross", 0, ln(1, 0, 1)), ("ffn", (a["ffn_w_gu"][0], a["ffn_w_down"][0]), ln(1, 0, 2)),
        ("odd", ln(1, 1, 0)), ("cross", 1, ln(1, 1, 1)), ("ffn", (a["ffn_w_gu"][1], a["ffn_w_down"][1]), ln(1, 1, 2)),
        ("hgrn", ln(2, 0, 0)), ("ffn", (a["ffn_w13_2"][0], a["ffn_w2_2"][0]), ln(2, 0, 1)),
        ("lru", ln(2, 1, 0)), ("ffn", (a["ffn_w13_2"][1], a["ffn_w2_2"][1]), ln(2, 1, 1)),
    ]


def kernel(**inputs):
    import concourse.bacc as bacc
    from concourse.bass_utils import run_bass_kernel_spmd

    nc = bacc.Bacc("TRN2", target_bir_lowering=False, num_devices=1)
    arrays = host_arrays({k: np.asarray(v) for k, v in inputs.items()})
    a = {k: nc.dram_tensor(k, v.shape, F32, kind="ExternalInput").ap() for k, v in arrays.items()}
    out = nc.dram_tensor("out", (S, D), F32, kind="ExternalOutput").ap()
    build(nc, a, out, all_stages(a))
    r = run_bass_kernel_spmd(nc, [arrays], core_ids=[0])
    return r.results[0]["out"].reshape(1, S, D)
```
